# Optimizing a Trainium2 kernel written in Bass

```python
import math
import jax, jax.numpy as jnp
from jax import lax
import numpy as np

D_MODEL = 1024
BATCH = 1
SEQ = 1024
DEPTH = 1
DEC_BATCH = 8
DEC_SEQ = 4
PAST_LEN = 2048
PAGE_SIZE = 128

NORM_EPS = 1e-6
SSD_D_INNER = D_MODEL
SSD_HEAD_DIM = 64
SSD_N_HEADS = SSD_D_INNER // SSD_HEAD_DIM
SSD_N_GROUPS = 4
SSD_D_STATE = 128
SSD_CONV = 4
SSD_CHUNK = 128
SSD_CONV_DIM = SSD_D_INNER + 2 * SSD_N_GROUPS * SSD_D_STATE
ATT_WINDOWS = (128, 512, 2048)
ATT_DILATIONS = (1, 4, 16)
ATT_N_GROUPS = 3
ATT_HEADS = 8
ATT_HEAD_DIM = 64
ATT_WIDTH = ATT_HEADS * ATT_HEAD_DIM
ROPE_DIM = ATT_HEAD_DIM // 4
ROPE_THETA = 500000.0
MEM_LEN = 256
MEM_HEADS = 4
MEM_HEAD_DIM = 128
MEM_WIDTH = MEM_HEADS * MEM_HEAD_DIM
N_BRANCHES = 3
IN_SIZES = (SSD_D_INNER, SSD_CONV_DIM, SSD_N_HEADS, ATT_N_GROUPS * 3 * ATT_WIDTH, ATT_WIDTH, MEM_WIDTH, MEM_WIDTH, N_BRANCHES * D_MODEL)
D_IN_PROJ = sum(IN_SIZES)
NEG_INF = -1e30

kernel_name = 'hybrid_ssd_dilated_attn_decoder_step'

def _rmsnorm(x, w):
    x32 = x.astype(jnp.float32)
    r = x32 * lax.rsqrt(jnp.mean(x32 * x32, axis=-1, keepdims=True) + NORM_EPS)
    return (r * w.astype(jnp.float32)).astype(x.dtype)

def _split_in(u):
    cuts = [int(c) for c in np.cumsum(IN_SIZES)[:-1]]
    return jnp.split(u, cuts, axis=-1)

def _rope(x, pos):
    half = ROPE_DIM // 2
    inv = jnp.power(ROPE_THETA, -jnp.arange(half, dtype=jnp.float32) * 2.0 / ROPE_DIM)
    ang = pos.astype(jnp.float32)[:, None] * inv[None, :]
    shape = (1, x.shape[1]) + (1,) * (x.ndim - 3) + (half,)
    cos = jnp.cos(ang).reshape(shape).astype(x.dtype)
    sin = jnp.sin(ang).reshape(shape).astype(x.dtype)
    x1, x2, rest = x[..., :half], x[..., half:ROPE_DIM], x[..., ROPE_DIM:]
    return jnp.concatenate([x1 * cos - x2 * sin, x2 * cos + x1 * sin, rest], axis=-1)

def _dilated_prompt(q, k, v, window, dil):
    b, s, h, dh = q.shape
    nk = window // dil
    length = s // dil
    nb = -(-length // nk)
    lp = nb * nk

    def to_blocks(a):
        a = a.reshape(b, length, dil, h, dh).transpose(0, 2, 1, 3, 4)
        a = jnp.pad(a, ((0, 0), (0, 0), (0, lp - length), (0, 0), (0, 0)))
        return a.reshape(b, dil, nb, nk, h, dh)

    def with_prev(a):
        prev = jnp.pad(a, ((0, 0), (0, 0), (1, 0), (0, 0), (0, 0), (0, 0)))[:, :, :nb]
        return jnp.concatenate([prev, a], axis=3)

    qb = to_blocks(q)
    kb = with_prev(to_blocks(k))
    vb = with_prev(to_blocks(v))
    sc = jnp.einsum('brnqhd,brnkhd->brnhqk', qb, kb, preferred_element_type=jnp.float32) * (dh ** -0.5)
    qi = jnp.arange(nk)[:, None]
    kj = jnp.arange(2 * nk)[None, :]
    rel = nk + qi - kj
    blk = jnp.arange(nb)[:, None, None]
    valid = (rel >= 0) & (rel <= nk) & ((blk - 1) * nk + kj >= 0)
    sc = jnp.where(valid[None, None, :, None], sc, NEG_INF)
    m = jnp.max(sc, axis=-1, keepdims=True)
    p = jnp.exp(sc - m)
    den = jnp.sum(p, axis=-1, keepdims=True)
    o = jnp.einsum('brnhqk,brnkhd->brnqhd', p.astype(v.dtype), vb, preferred_element_type=jnp.float32)
    o = o / jnp.swapaxes(den, 3, 4)
    lse = jnp.swapaxes((m + jnp.log(den))[..., 0], 3, 4)

    def from_blocks(a):
        a = a.reshape((b, dil, lp) + a.shape[4:])[:, :, :length]
        a = jnp.moveaxis(a, 1, 2)
        return a.reshape((b, s) + a.shape[3:])

    return from_blocks(o), from_blocks(lse)

def _dilated_sample(q, kv_new, buf, window, dil):
    b, t, h, dh = q.shape
    nk = window // dil
    wb = buf.shape[1]
    idx = wb + jnp.arange(t)[:, None] - dil * jnp.arange(nk + 1)[None, :]
    valid = idx >= 0
    kv_old = buf[:, jnp.clip(idx, 0, wb - 1)]
    kv_cur = kv_new.astype(buf.dtype)[:, jnp.clip(idx - wb, 0, t - 1)]
    kv_g = jnp.where((idx >= wb)[None, :, :, None, None, None], kv_cur, kv_old)
    sc = jnp.einsum('bthd,btkhd->bthk', q, kv_g[:, :, :, 0], preferred_element_type=jnp.float32) * (dh ** -0.5)
    sc = jnp.where(valid[None, :, None, :], sc, NEG_INF)
    m = jnp.max(sc, axis=-1, keepdims=True)
    p = jnp.exp(sc - m)
    den = jnp.sum(p, axis=-1, keepdims=True)
    o = jnp.einsum('bthk,btkhd->bthd', p.astype(kv_g.dtype), kv_g[:, :, :, 1], preferred_element_type=jnp.float32) / den
    lse = (m + jnp.log(den))[..., 0]
    return o, lse

def _mem_kv(mem, mem_norm_w, w_mem_kv):
    b, m, _ = mem.shape
    return (_rmsnorm(mem, mem_norm_w) @ w_mem_kv).reshape(b, m, 2, MEM_HEADS, MEM_HEAD_DIM)

def _mem_attn(q, kv):
    b, t = q.shape[0], q.shape[1]
    sc = jnp.einsum('bthd,bmhd->bhtm', q, kv[:, :, 0], preferred_element_type=jnp.float32) * (MEM_HEAD_DIM ** -0.5)
    p = jax.nn.softmax(sc, axis=-1)
    o = jnp.einsum('bhtm,bmhd->bthd', p.astype(kv.dtype), kv[:, :, 1])
    return o.reshape(b, t, MEM_WIDTH)

def _ssd_scan(x, dt, a_neg, bm, cm, init_state):
    b, t, h, p = x.shape
    g, n = bm.shape[2], bm.shape[3]
    e = h // g
    q = min(SSD_CHUNK, t)
    nc = -(-t // q)
    pad = nc * q - t

    def padf(a):
        return jnp.pad(a, ((0, 0), (0, pad)) + ((0, 0),) * (a.ndim - 2))

    x, dt, bm, cm = padf(x), padf(dt), padf(bm), padf(cm)
    xdt = (x * dt[..., None]).reshape(b, nc, q, g, e, p)
    acs = jnp.cumsum((dt * a_neg).reshape(b, nc, q, g, e), axis=2)
    bm = bm.reshape(b, nc, q, g, n)
    cm = cm.reshape(b, nc, q, g, n)
    diff = acs[:, :, :, None] - acs[:, :, None, :]
    tril = jnp.tril(jnp.ones((q, q), dtype=bool))[None, None, :, :, None, None]
    lmat = jnp.exp(jnp.where(tril, diff, -jnp.inf))
    cb = jnp.einsum('bclgn,bcsgn->bclsg', cm, bm)
    y_diag = jnp.einsum('bclsg,bclsge,bcsgep->bclgep', cb, lmat, xdt)
    decay_out = jnp.exp(acs[:, :, -1:] - acs)
    st = jnp.einsum('bclgn,bclge,bclgep->bcgepn', bm, decay_out, xdt)
    chunk_decay = jnp.exp(acs[:, :, -1])

    def step(s, inp):
        dec, add = inp
        return s * dec[..., None, None] + add, s

    final, prev = lax.scan(step, init_state.reshape(b, g, e, p, n),
                           (chunk_decay.transpose(1, 0, 2, 3), st.transpose(1, 0, 2, 3, 4, 5)))
    prev = prev.transpose(1, 0, 2, 3, 4, 5)
    y_off = jnp.einsum('bclgn,bcgepn,bclge->bclgep', cm, prev, jnp.exp(acs))
    y = (y_diag + y_off).reshape(b, nc * q, h, p)[:, :t]
    return y, final.reshape(b, h, p, n)

def _ssd_branch(z, xbc, dt_raw, conv_prev, ssm_prev, conv_w, conv_b, dt_bias, a_log, d_skip, ssd_norm_w):
    b, t, _ = xbc.shape
    xp = jnp.concatenate([conv_prev.astype(xbc.dtype), xbc], axis=1)
    acc = conv_b + xp[:, 0:t] * conv_w[0]
    for kk in range(1, SSD_CONV):
        acc = acc + xp[:, kk:kk + t] * conv_w[kk]
    xc = jax.nn.silu(acc)
    new_conv = xp[:, xp.shape[1] - (SSD_CONV - 1):]
    gn = SSD_N_GROUPS * SSD_D_STATE
    xs = xc[..., :SSD_D_INNER].reshape(b, t, SSD_N_HEADS, SSD_HEAD_DIM).astype(jnp.float32)
    bm = xc[..., SSD_D_INNER:SSD_D_INNER + gn].reshape(b, t, SSD_N_GROUPS, SSD_D_STATE).astype(jnp.float32)
    cm = xc[..., SSD_D_INNER + gn:].reshape(b, t, SSD_N_GROUPS, SSD_D_STATE).astype(jnp.float32)
    dt = jax.nn.softplus(dt_raw.astype(jnp.float32) + dt_bias.astype(jnp.float32))
    a_neg = -jnp.exp(a_log.astype(jnp.float32))
    y, new_ssm = _ssd_scan(xs, dt, a_neg, bm, cm, ssm_prev.astype(jnp.float32))
    y = y + d_skip.astype(jnp.float32)[:, None] * xs
    y = y.reshape(b, t, SSD_D_INNER).astype(z.dtype)
    y = _rmsnorm(y * jax.nn.silu(z), ssd_norm_w)
    return y, new_conv, new_ssm.astype(ssm_prev.dtype)

def _layer(x, pos0, mem_kv, conv_prev, ssm_prev, win_bufs, norm_in_w, w_in, conv_w, conv_b, dt_bias, a_log,
           d_skip, ssd_norm_w, w_br_ssd, w_br_att, w_br_mem, w_out, norm_f_w):
    b, t, _ = x.shape
    h = _rmsnorm(x, norm_in_w)
    u = h @ w_in
    z_ssd, xbc, dt_raw, qkv, z_att, q_mem, z_mem, gate_raw = _split_in(u)
    y_ssd, new_conv, new_ssm = _ssd_branch(z_ssd, xbc, dt_raw, conv_prev, ssm_prev, conv_w, conv_b,
                                           dt_bias, a_log, d_skip, ssd_norm_w)
    qkv = qkv.reshape(b, t, ATT_N_GROUPS, 3, ATT_HEADS, ATT_HEAD_DIM)
    pos = pos0 + jnp.arange(t)
    q = _rope(qkv[:, :, :, 0], pos)
    k = _rope(qkv[:, :, :, 1], pos)
    v = qkv[:, :, :, 2]
    kv = jnp.stack([k, v], axis=3)
    outs, lses, new_win = [], [], []
    for gi in range(ATT_N_GROUPS):
        w, d = ATT_WINDOWS[gi], ATT_DILATIONS[gi]
        if win_bufs is None:
            o, l = _dilated_prompt(q[:, :, gi], k[:, :, gi], v[:, :, gi], w, d)
            new_win.append(kv[:, t - min(w, t):, gi])
        else:
            o, l = _dilated_sample(q[:, :, gi], kv[:, :, gi], win_bufs[gi], w, d)
            new_win.append(kv[:, :, gi])
        outs.append(o)
        lses.append(l)
    wts = jax.nn.softmax(jnp.stack(lses), axis=0)
    o_att = jnp.sum(wts[..., None] * jnp.stack(outs), axis=0).reshape(b, t, ATT_WIDTH).astype(x.dtype)
    y_att = o_att * jax.nn.silu(z_att)
    y_mem = _mem_attn(q_mem.reshape(b, t, MEM_HEADS, MEM_HEAD_DIM), mem_kv).astype(x.dtype) * jax.nn.silu(z_mem)
    gates = jax.nn.sigmoid(gate_raw).reshape(b, t, N_BRANCHES, D_MODEL)
    merged = (gates[:, :, 0] * (y_ssd @ w_br_ssd) + gates[:, :, 1] * (y_att @ w_br_att)
              + gates[:, :, 2] * (y_mem @ w_br_mem))
    y = _rmsnorm(x + merged @ w_out, norm_f_w)
    return y, new_win, new_conv, new_ssm

def setup_inputs(seed: int = 0) -> dict:
    key = jax.random.key(seed)
    ks = jax.random.split(key, 32)
    f32 = jnp.float32

    def nrm(k, shape, scale):
        return scale * jax.random.normal(k, shape, f32)

    dt0 = jnp.exp(jax.random.uniform(ks[0], (SSD_N_HEADS,), f32, math.log(1e-3), math.log(1e-1)))
    win_shape = lambda w: (DEC_BATCH, min(w, PAST_LEN), 2, ATT_HEADS, ATT_HEAD_DIM)
    return {
        'x_prompt': nrm(ks[1], (BATCH, SEQ, D_MODEL), 1.0),
        'x_sample': nrm(ks[2], (DEC_BATCH, DEC_SEQ, D_MODEL), 1.0),
        'mem_prompt': nrm(ks[3], (BATCH, MEM_LEN, D_MODEL), 1.0),
        'cache_win128_kv': nrm(ks[4], win_shape(ATT_WINDOWS[0]), 1.0),
        'cache_win512_kv': nrm(ks[5], win_shape(ATT_WINDOWS[1]), 1.0),
        'cache_win2048_kv': nrm(ks[6], win_shape(ATT_WINDOWS[2]), 1.0),
        'cache_mem_kv': nrm(ks[7], (DEC_BATCH, MEM_LEN, 2, MEM_HEADS, MEM_HEAD_DIM), 1.0),
        'state_conv': nrm(ks[8], (DEC_BATCH, SSD_CONV - 1, SSD_CONV_DIM), 1.0),
        'state_ssm': nrm(ks[9], (DEC_BATCH, SSD_N_HEADS, SSD_HEAD_DIM, SSD_D_STATE), 0.1),
        'norm_in_w': 1.0 + nrm(ks[10], (D_MODEL,), 0.02),
        'w_in': nrm(ks[11], (D_MODEL, D_IN_PROJ), D_MODEL ** -0.5),
        'conv_w': nrm(ks[12], (SSD_CONV, SSD_CONV_DIM), SSD_CONV ** -0.5),
        'conv_b': nrm(ks[13], (SSD_CONV_DIM,), 0.01),
        'dt_bias': dt0 + jnp.log(-jnp.expm1(-dt0)),
        'a_log': jnp.log(jax.random.uniform(ks[14], (SSD_N_HEADS,), f32, 1.0, 16.0)),
        'd_skip': 1.0 + nrm(ks[15], (SSD_N_HEADS,), 0.1),
        'ssd_norm_w': 1.0 + nrm(ks[16], (SSD_D_INNER,), 0.02),
        'mem_norm_w': 1.0 + nrm(ks[17], (D_MODEL,), 0.02),
        'w_mem_kv': nrm(ks[18], (D_MODEL, 2 * MEM_WIDTH), D_MODEL ** -0.5),
        'w_br_ssd': nrm(ks[19], (SSD_D_INNER, D_MODEL), SSD_D_INNER ** -0.5),
        'w_br_att': nrm(ks[20], (ATT_WIDTH, D_MODEL), ATT_WIDTH ** -0.5),
        'w_br_mem': nrm(ks[21], (MEM_WIDTH, D_MODEL), MEM_WIDTH ** -0.5),
        'w_out': nrm(ks[22], (D_MODEL, D_MODEL), D_MODEL ** -0.5),
        'norm_f_w': 1.0 + nrm(ks[23], (D_MODEL,), 0.02),
    }

def reference(x_prompt, x_sample, mem_prompt, cache_win128_kv, cache_win512_kv, cache_win2048_kv, cache_mem_kv,
              state_conv, state_ssm, norm_in_w, w_in, conv_w, conv_b, dt_bias, a_log, d_skip, ssd_norm_w,
              mem_norm_w, w_mem_kv, w_br_ssd, w_br_att, w_br_mem, w_out, norm_f_w):
    bp = x_prompt.shape[0]
    p_mem_kv = _mem_kv(mem_prompt, mem_norm_w, w_mem_kv)
    conv0 = jnp.zeros((bp, SSD_CONV - 1, SSD_CONV_DIM), x_prompt.dtype)
    ssm0 = jnp.zeros((bp, SSD_N_HEADS, SSD_HEAD_DIM, SSD_D_STATE), jnp.float32)
    y_prompt, p_win, p_conv, p_ssm = _layer(
        x_prompt, 0, p_mem_kv, conv0, ssm0, None, norm_in_w, w_in, conv_w, conv_b, dt_bias, a_log, d_skip,
        ssd_norm_w, w_br_ssd, w_br_att, w_br_mem, w_out, norm_f_w)
    y_sample, s_win, s_conv, s_ssm = _layer(
        x_sample, PAST_LEN, cache_mem_kv, state_conv, state_ssm, (cache_win128_kv, cache_win512_kv, cache_win2048_kv),
        norm_in_w, w_in, conv_w, conv_b, dt_bias, a_log, d_skip, ssd_norm_w, w_br_ssd, w_br_att, w_br_mem,
        w_out, norm_f_w)
    return (y_prompt, y_sample, p_win[0], p_win[1], p_win[2], p_mem_kv, p_conv, p_ssm,
            s_win[0], s_win[1], s_win[2], s_conv, s_ssm)


_drawn_inputs = setup_inputs


def setup_inputs(seed=0):
    import zlib

    import numpy as np

    out = dict(_drawn_inputs(seed))
    spreads = {}
    factors = {'cache_win128_kv': 4.024,
     'cache_win512_kv': 4.073,
     'cache_win2048_kv': 4.138,
     'conv_b': 2.952,
     'd_skip': 3.055,
     'ssd_norm_w': 18.303,
     'mem_norm_w': 8.283,
     'norm_f_w': 8.414,
     'cache_mem_kv': 5.628}
    for name, (base, spread) in spreads.items():
        noise = np.random.default_rng([zlib.crc32(name.encode()), seed]).standard_normal(out[name].shape)
        drawn = base * np.exp(spread * noise) if base else spread * noise
        out[name] = __import__('jax').numpy.asarray(drawn.astype(out[name].dtype))
    for name, factor in factors.items():
        out[name] = (out[name] * factor).astype(out[name].dtype)
    return out
```

```python
from contextlib import ExitStack

import numpy as np
import concourse.bass as bass
from concourse import mybir

F32 = mybir.dt.float32
F32R = mybir.dt.float32r
ALU = mybir.AluOpType
ACT = mybir.ActivationFunctionType
AX = mybir.AxisListType.X

P = 128
D = 1024
KT8 = D // P
SEQ = 1024
NB = SEQ // P
BS, TS = 8, 4
NS = BS * TS
TOK = SEQ + NS
MEM = 256
HEADS, HD = 8, 64
AW = HEADS * HD
MH, MD = 4, 128
GROUPS = ((128, 1), (512, 4), (2048, 16))
NG = len(GROUPS)
SH, SP, SG, SN = 16, 64, 4, 128
CONV = 4
CD = D + 2 * SG * SN
C_Z, C_XBC, C_DT = 0, D, D + CD
C_QKV = C_DT + SH
C_ZATT = C_QKV + NG * 3 * AW
C_QMEM = C_ZATT + AW
C_ZMEM = C_QMEM + MH * MD
C_GATE = C_ZMEM + MH * MD
EPS = 1e-6
CW = 256
THIRD = TOK // 3
OROW = AW + 2 * HEADS
NFT = 48
FT_XBC, FT_GATE, FT_QMEM, FT_ZMEM = 0, 16, 40, 44


def constants():
    i = np.arange(P)
    ident = (i[:, None] == i[None, :]).astype(np.float32)
    neg = np.float32(-1e30)
    prev = np.where(i[None, :] >= i[:, None], np.float32(0), neg)
    diag = np.where(i[None, :] <= i[:, None], np.float32(0), neg)
    same = (i[:, None] % 2) == (i[None, :] % 2)
    two = np.where(same & (i[None, :] <= i[:, None]), np.float32(0), neg)
    upper = (i[:, None] <= i[None, :]).astype(np.float32)
    pos = np.zeros((P, 3 * NB + 1), np.int64)
    for b in range(NB):
        pos[:, b] = P * b + i
        pos[:, NB + b] = b // 2 + 4 * (P * (b % 2) + i)
        pos[:, 2 * NB + b] = 8 * i + b
    pos[:, 3 * NB] = 2048 + i % TS
    inv = np.power(np.float32(500000.0), -np.arange(8, dtype=np.float32) * np.float32(2.0) / np.float32(16))
    ang = pos.astype(np.float32)[:, :, None] * inv[None, None, :].astype(np.float32)
    cos, sin = np.cos(ang).astype(np.float32), np.sin(ang).astype(np.float32)
    rope = np.concatenate([cos, cos, -sin, sin], -1).reshape(P, -1)
    s = np.arange(P)
    upper_s = ((s[:, None] // TS == s[None, :] // TS) & (s[:, None] <= s[None, :])).astype(np.float32)[:, :NS]
    same_b = (s[:, None] // TS == np.arange(BS)[None, :]).astype(np.float32)
    same_s = (s[:, None] // TS == np.arange(NS)[None, :] // TS).astype(np.float32)
    ones = np.ones((P, P), np.float32)
    t_of = (i // HEADS) % TS
    old = np.where(i[None, :] >= t_of[:, None], np.float32(0), neg)
    new = []
    for half in range(2):
        b_of = 4 * half + i // 32
        kb, kt = np.arange(NS) // TS, np.arange(NS) % TS
        mine = kb[None, :] == b_of[:, None]
        new.append(np.where(mine & (kt[None, :] <= t_of[:, None]), np.float32(0), neg))
        new.append(np.where(mine & (kt[None, :] == t_of[:, None]), np.float32(0), neg))
    parts = dict(ident=ident, prev=prev, diag=diag, two=two, upper=upper, rope=rope, upper_s=upper_s,
                 same_b=same_b, same_s=same_s, ones=ones, old=old, new=np.concatenate(new, 1))
    at, offset = {}, 0
    for name, a in parts.items():
        at[name] = (offset, offset + a.shape[1])
        offset += a.shape[1]
    return np.ascontiguousarray(np.concatenate(list(parts.values()), 1), dtype=np.float32), at


CONST, CONST_AT = constants()
NCONST = CONST.shape[1]
NAMES = ['x_prompt', 'x_sample', 'mem_prompt', 'cache_win128_kv', 'cache_win512_kv', 'cache_win2048_kv',
         'cache_mem_kv', 'state_conv', 'state_ssm', 'norm_in_w', 'w_in', 'conv_w', 'conv_b', 'dt_bias', 'a_log',
         'd_skip', 'ssd_norm_w', 'mem_norm_w', 'w_mem_kv', 'w_br_ssd', 'w_br_att', 'w_br_mem', 'w_out', 'norm_f_w']


def plan():
    chunks, sched = [], []

    def chunk(kind, detail, src, col):
        chunks.append((kind, detail, src, col))
        return len(chunks) - 1

    mem_chunks = [chunk("mk", i, "w_mem_kv", CW * i) for i in range(2)]
    mem_chunks += [chunk("mv", i, "w_mem_kv", 512 + CW * i) for i in range(2)]
    qm = [chunk("feat", FT_QMEM + 2 * i, "w_in", C_QMEM + CW * i) for i in range(2)]
    zm = [chunk("feat", FT_ZMEM + 2 * i, "w_in", C_ZMEM + CW * i) for i in range(2)]
    fill_src = [("feat", FT_XBC + 2 * i, "w_in", C_XBC + CW * i) for i in range(8)]
    fill_src += [("z", i, "w_in", C_Z + CW * i) for i in range(4)]
    fill_src += [("za", i, "w_in", C_ZATT + CW * i) for i in range(2)]
    fill_src += [("feat", FT_GATE + 2 * i, "w_in", C_GATE + CW * i) for i in range(12)]

    def project(n):
        kind = chunks[n][0]
        if kind in ("mk", "mv"):
            steps = [("tok", n, t) for t in range(MEM // P)]
            if kind == "mk":
                steps = [steps[0], steps[1], ("turn", n, 0), ("turn", n, 1)]
        elif kind in ("q", "k"):
            steps = []
            for t in range(NB + 1):
                steps.append(("tok", n, t))
                if t >= 2:
                    steps.append(("turn", n, t - 2))
            steps.append(("turn", n, NB - 1))
        elif kind == "feat":
            steps = [("feat", n, f, j) for f in range(2) for j in range(3)]
        else:
            steps = [("tok", n, t) for t in range(NB + 1)]
        return steps

    units = []

    def unit(*u):
        units.append(u)
        return len(units) - 1

    def beside(todo, fillers):
        steps = []
        for n in fillers:
            steps += project(n) + [("split", n)]
        stages = []
        for a in todo:
            stages.append([("scores", a), ("softmax", a), ("ptrans", a), ("pv", a)])
        side = []
        for i in range(len(todo) + 1):
            if i < len(todo):
                side += [stages[i][0], stages[i][1]]
            if i >= 1:
                side += [stages[i - 1][2], stages[i - 1][3]]
        out, done = [], 0
        groups = [side[j:j + 2] for j in range(0, len(side), 2)]
        for i, s in enumerate(steps):
            out.append(s)
            upto = len(groups) * (i + 1) // max(len(steps), 1)
            while done < upto:
                out.extend(groups[done])
                done += 1
        for g in groups[done:]:
            out.extend(g)
        return out

    sched += [("norm_a", 0), ("norm_a", 1), ("norm_b", 0), ("norm_a", 2), ("norm_b", 1), ("split0", 0), ("split0", 1)]
    sched += [("norm_a", 3), ("norm_b", 2)]
    i = 4
    for n in mem_chunks:
        for s in project(n) + [("split", n)]:
            sched.append(s)
            if i < 11 and s[0] == "tok":
                sched += [("norm_a", i), ("norm_b", i - 1)]
                i += 1
    assert i == 11
    sched += [("norm_b", 10), ("dt",)]
    for n in qm + zm:
        sched += project(n) + [("split", n)]
    fillers = []

    def take(k):
        got = []
        for _ in range(k):
            if fill_src:
                got.append(chunk(*fill_src.pop(0)))
        return got

    sched += beside([unit("mem", t) for t in range(NB)], take(4))
    for g in range(NG):
        qkv = [chunk(k, (g, i), "w_in", C_QKV + g * 3 * AW + j * AW + CW * i)
               for j, k in enumerate("qkv") for i in range(2)]
        for n in qkv:
            sched += project(n) + [("split", n)]
        k = 8 if g < NG - 1 else len(fill_src)
        k = {0: 7, 1: 7, 2: len(fill_src)}[g]
        sched += beside([unit("att", g, b, h) for b in range(NB) for h in range(2)], take(k))
    sched += [("merge", b) for b in range(NB)]
    sched += [("sprep", g) for g in range(NG)]
    sets = []
    for b in range(BS):
        sets.append(("att", b, 0, None))
        for g in (1, 2):
            sets += [("att", b, g, t) for t in range(TS)]
    sets += [("mem", b, k, None) for b in range(BS) for k in range(MEM // P)]
    sched += [("skey", n) for n in range(len(sets) + 1)]
    sched += [("ssoft", "att"), ("ssoft", "mem")]
    sched += [("sval", n) for n in range(len(sets))]
    sched += [("sout",), ("ssd_setup",)] + [("ya", k) for k in range(KT8)]
    p1 = []
    for i in range(4):
        n = chunk("p1", 2 * i, "att+mem", CW * i)
        p1 += [("p1", n, f, br, j) for f in range(2) for br in range(2) for j in range(3)] + [("split", n)]
    done = 0
    for c in range(NB):
        for q in range(6):
            sched.append(("ssd", c, q))
            upto = len(p1) * (6 * c + q + 1) // (6 * NB)
            while done < upto:
                sched.append(p1[done])
                done += 1
    sched += [("ssd_state",), ("ssd", NB, 0), ("ssd_s",)] + [("ssd", NB, q) for q in (1, 2, 3)]
    sched += [("ssd_sb", b) for b in range(BS)] + [("ssd", NB, 4), ("ssd", NB, 5), ("tail",)]
    sched += [("yb", k) for k in range(KT8)]
    for i in range(4):
        n = chunk("p2", 2 * i, "w_br_ssd", CW * i)
        sched += [("p2", n, f, j) for f in range(2) for j in range(3)] + [("split", n)]
    for i in range(4):
        n = chunk("out", i, "w_out", CW * i)
        sched += [("out", n, t) for t in range(NB + 1)] + [("split", n)]
    return chunks, sched, units, sets


def build_program(nc, io, outs):
    chunks, sched, units, sets = plan()
    n_chunks = len(chunks)
    order = {}
    kinds = {}
    for s in sched:
        order[s] = kinds.setdefault(s[0], 0)
        kinds[s[0]] += 1
    proj = {}
    for s in sched:
        if s[0] in ("tok", "feat", "p1", "p2", "out"):
            proj[s] = len(proj)
    n_act_proj = sum(s[0] in ("tok", "feat") for s in sched)
    slot_of, slot_stores, turned = {}, [], {}
    for s in sched:
        if s[0] != "tok":
            continue
        _, n, t = s
        kind, detail = chunks[n][0], chunks[n][1]
        if kind == "mv" or (kind == "v" and t < NB):
            continue
        slot_of[s] = len(slot_of)
        if kind == "mk" or kind in ("z", "za") or (kind == "q" and t == NB):
            stores = 1
        elif t == NB:
            stores = 2
        elif kind == "q":
            stores = 0
        else:
            g = detail[0]
            stores = ((t == NB - 1), (t % 2), 1)[g]
        slot_stores.append(int(stores))
    for s in sched:
        if s[0] == "turn":
            turned[s] = len(turned)
    turn_of_slot = {slot_of[("tok", s[1], s[2])]: v for s, v in turned.items()}
    roped = {}
    for s in sched:
        if s[0] == "tok" and chunks[s[1]][0] in ("q", "k"):
            roped[s] = len(roped)
    stored_before = [[0] * 4]
    for c, k in enumerate(slot_stores):
        row = list(stored_before[-1])
        row[c % 4] += k
        stored_before.append(row)
    feats = [s for s in sched if s[0] == "feat"]
    feat_no = {}
    for s in feats:
        feat_no.setdefault((s[1], s[2]), len(feat_no))
    is_conv = {k: chunks[k[0]][1] < FT_GATE for k in feat_no}
    conv_no = {}
    for k in feat_no:
        if is_conv[k]:
            conv_no[k] = len(conv_no)
    o_use, o_count = {}, 0
    for a, u in enumerate(units):
        if u[0] == "mem" or u[3] == 0:
            o_count += 1
        o_use[a] = o_count - 1
    n_mem = sum(u[0] == "mem" for u in units)
    first_att = {g: min(a for a, u in enumerate(units) if u[0] == "att" and u[1] == g) for g in range(NG)}

    with ExitStack() as ctx:
        def sem(name):
            return ctx.enter_context(nc.semaphore(name))

        def sb(stack, name, shape, dt=F32):
            return stack.enter_context(nc.sbuf_tensor(name, shape, dt))

        def dram(name, shape):
            return nc.dram_tensor(name, shape, F32, kind="Internal").ap()

        featT = dram("feat_T", [NFT, P, TOK])
        zrow = dram("z_rows", [TOK, D])
        zarow = dram("z_att_rows", [TOK, AW])
        qkv_s = dram("qkv_sample", [NS, NG * 3 * AW])
        orow = [dram(f"o_rows{g}", [SEQ, OROW]) for g in range(NG)]
        yT = dram("y_T", [16, P, TOK])
        tailT = dram("tail_T", [16, P, 35])
        accT = dram("acc_T", [KT8, P, TOK])

        bank = [ctx.enter_context(nc.psum_tensor(f"bank{i}", [P, 512], F32)) for i in range(8)]

        con = sb(ctx, "con", [P, NCONST])

        def table(name):
            a, b = CONST_AT[name]
            return con[:, a:b]

        w_raw = sb(ctx, "w_raw", [P, KT8, CW])
        w_hi = sb(ctx, "w_hi", [P, 2, KT8, CW], F32R)
        w_lo = sb(ctx, "w_lo", [P, 2, KT8, CW], F32R)
        small = sb(ctx, "small", [P, 64])
        dtv = sb(ctx, "dtv", [P, 9 * SH])
        hrow = sb(ctx, "hrow", [P, 3, SH])

        stage = ExitStack()
        rows = sb(stage, "rows", [P, 4, CW])
        fstage = sb(stage, "fstage", [P, 2, TOK])
        fraw = sb(stage, "fraw", [P, 3 + SEQ + BS * (TS + 3)])
        soft = sb(stage, "soft", [P, 2, 4, CW])
        softT = sb(stage, "softT", [P, 2, 4, 2, P])
        obuf = sb(stage, "obuf", [P, 2, OROW])
        nmax = sb(stage, "nmax", [P, 2, 4])
        mstat = sb(stage, "mstat", [P, 2, 12])
        wdt_raw = sb(stage, "wdt_raw", [P, KT8, SH])
        wdt_hi = sb(stage, "wdt_hi", [P, KT8, SH], F32R)
        wdt_lo = sb(stage, "wdt_lo", [P, KT8, SH], F32R)
        convw = sb(stage, "convw", [P, 80])
        cstate = sb(stage, "cstate", [P, 16, 24])
        hTh = sb(stage, "hT_hi", [P, KT8, TOK], F32R)
        hTl = sb(stage, "hT_lo", [P, KT8, TOK], F32R)

        area = ExitStack()
        xin = sb(area, "xin", [P, 2, D])
        normw = sb(area, "normw", [P, 2, D])
        xsq = sb(area, "xsq", [P, D])
        memTh = sb(area, "memT_hi", [P, KT8, MEM], F32R)
        memTl = sb(area, "memT_lo", [P, KT8, MEM], F32R)
        KmT = sb(area, "KmT", [P, MH, MEM])
        Vm = sb(area, "Vm", [P, 2, MH * MD])
        area.close()
        area = ExitStack()
        qmem = sb(area, "qmem", [P, 2, MH, P])
        zmem = sb(area, "zmem", [P, 2, MH, P])
        area.close()
        area = ExitStack()
        QT = sb(area, "QT", [P, 4, SEQ])
        KTt = sb(area, "KT", [P, 4, SEQ])
        V = sb(area, "V", [P, NB, AW])
        area.close()
        area = ExitStack()
        mo = sb(area, "mo", [P, 2, NG, OROW])
        mz = sb(area, "mz", [P, 2, AW])
        macc = sb(area, "macc", [P, 2, AW])
        mtmp = sb(area, "mtmp", [P, AW])
        mst = sb(area, "mst", [P, 2, AW])
        mw = sb(area, "mw", [P, 128])
        area.close()
        NRING = 6
        area = ExitStack()
        kvring = sb(area, "kvring", [P, NRING, AW])
        vS = sb(area, "vS", [NS, NG, AW])
        qkS = sb(area, "qkS", [NS, 2, AW])
        qbd = sb(area, "qbd", [P, NG, 4, NS, 2])
        kTs = sb(area, "kTs", [P, NG, 4, NS])
        kset = sb(area, "kset", [P, 2, 4, P])
        sT = sb(area, "sT", [P, NG, 256])
        sTn = sb(area, "sTn", [NS, NG, 256])
        srow = sb(area, "srow", [P, 2, NG, P + NS])
        pT = sb(area, "pT", [P, NG, 2, P])
        pTn = sb(area, "pTn", [NS, NG, 2, P])
        area.close()
        mq = fstage[:, 0, 0:MH * NS].rearrange("p (h n) -> p h n", h=MH)
        mzs = fstage[:, 0, 256:256 + MH * NS].rearrange("p (h n) -> p h n", h=MH)
        zas = fstage[:, 0, 512:512 + AW]
        ysam = fstage[:, 1, 0:2 * 4 * NS].rearrange("p (a h n) -> p a h n", a=2, h=4)
        mS = soft[:, 0, 0, :]
        mrow = soft[:, 0, 1, :]
        mP = soft[:, 0, 2, :]
        sstat = soft[:, 0, 3, 0:16]
        stage.close()

        late = ExitStack()
        yAh = sb(late, "y_am_hi", [P, KT8, TOK], F32R)
        yAl = sb(late, "y_am_lo", [P, KT8, TOK], F32R)
        ssd = ExitStack()
        yraw = sb(ssd, "yraw", [P, TOK])
        gate1 = sb(ssd, "gate1", [P, 2, TOK])
        acc1 = sb(ssd, "acc1", [P, TOK])
        xc = sb(ssd, "xc", [P, 16, P])
        zt = sb(ssd, "zt", [P, D])
        xtok = sb(ssd, "xtok", [P, D])
        xdt = sb(ssd, "xdt", [P, D])
        xdec = sb(ssd, "xdec", [P, D])
        btok = sb(ssd, "btok", [P, SG * SN])
        Lm = sb(ssd, "Lm", [P, SH, P])
        CBm = sb(ssd, "CBm", [P, SG, P])
        state = sb(ssd, "state", [P, D])
        yy = sb(ssd, "yy", [P, D])
        yo = sb(ssd, "yo", [P, D])
        yst = sb(ssd, "yst", [P, KT8, P])
        yst2 = sb(ssd, "yst2", [P, KT8, NS])
        ssdw = sb(ssd, "ssdw", [P, D])
        sc = sb(ssd, "sc", [P, 10, 9 * SH])
        ssd.close()
        last = ExitStack()
        yBh = sb(last, "y_s_hi", [P, KT8, TOK], F32R)
        yBl = sb(last, "y_s_lo", [P, KT8, TOK], F32R)
        gate2 = sb(last, "gate2", [P, TOK])
        acc2 = sb(last, "acc2", [P, TOK])
        yraw2 = sb(last, "yraw2", [P, TOK])
        last.close()
        late.close()
        late = ExitStack()
        mTh = sb(late, "m_hi", [P, KT8, TOK], F32R)
        mTl = sb(late, "m_lo", [P, KT8, TOK], F32R)
        orows = sb(late, "orows", [P, NB + 1, D])
        xres = sb(late, "xres", [P, 8, CW])
        normf = sb(late, "normf", [P, D])
        osq = sb(late, "osq", [P, D])
        late.close()

        s_const = sem("s_const")
        s_x = [sem(f"s_x{i}") for i in range(2)]
        s_sq = sem("s_sq")
        s_xn = sem("s_xn")
        s_var = sem("s_var")
        s_rstd = sem("s_rstd")
        s_xt = sem("s_xt")
        s_hhi = sem("s_hhi")
        s_hlo = sem("s_hlo")
        s_w = sem("s_w")
        s_whi = sem("s_whi")
        s_wlo = sem("s_wlo")
        s_wused = sem("s_wused")
        s_pj = sem("s_pj")
        s_pjev = sem("s_pjev")
        s_row = [sem(f"s_row{i}") for i in range(4)]
        s_rope = sem("s_rope")
        s_turn = sem("s_turn")
        s_turned = sem("s_turned")
        s_fst = [sem(f"s_fst{i}") for i in range(2)]
        s_conv = sem("s_conv")
        s_silu = sem("s_silu")
        s_vst = sem("s_vst")
        s_sc = sem("s_sc")
        s_msk = sem("s_msk")
        s_max = sem("s_max")
        s_exp = sem("s_exp")
        s_pn = sem("s_pn")
        s_pt = sem("s_pt")
        s_ptA = sem("s_ptA")
        s_ptD = sem("s_ptD")
        s_pv = sem("s_pv")
        s_o = sem("s_o")
        s_ost = [sem(f"s_ost{i}") for i in range(2)]
        s_qm = [sem(f"s_qm{i}") for i in range(2)]
        s_dve = sem("s_dve")
        s_act = sem("s_act")
        s_wdt = sem("s_wdt")
        s_wdth = sem("s_wdth")
        s_wdtl = sem("s_wdtl")
        s_dtp = sem("s_dtp")
        s_dte = sem("s_dte")
        s_tail = sem("s_tail")
        s_cv = sem("s_cv")
        s_cvt = sem("s_cvt")
        s_cvc = sem("s_cvc")

        def wsrc(n):
            _, _, src, col = chunks[n]
            if src == "att+mem":
                halves = [io["w_br_att"][:, col:col + CW], io["w_br_mem"][:, col:col + CW]]
            else:
                halves = [io[src][512 * i:512 * i + 512, col:col + CW] for i in range(2)]
            return [a.rearrange("(k p) n -> p k n", p=P) for a in halves]

        def token_cols(buf, k, g, b):
            if g == 0:
                return buf[:, k, P * b:P * b + P]
            if g == 1:
                lo = b // 2 + 512 * (b % 2)
                return buf[:, k, lo:lo + 4 * 127 + 1:4]
            return buf[:, k, b:b + 8 * 127 + 1:8]

        def kv_rows(g, b, kv, c0, n):
            out = outs[2 + g].rearrange("a t s h d -> (a t) s (h d)")[:, kv, c0:c0 + n]
            if g == 0:
                return [(0, P, out)] if b == NB - 1 else []
            if g == 1:
                return [(0, P, out.rearrange("(i r) c -> r i c", r=4)[b // 2])] if b % 2 else []
            return [(0, P, out.rearrange("(i r) c -> r i c", r=8)[b])]

        def feat_done_stores(k):
            return 16 * (k // 2)

        def norm_src(i):
            if i < 2:
                return io["mem_prompt"].rearrange("a (n p) d -> (a n) p d", p=P)[i], P
            if i < 10:
                return io["x_prompt"].rearrange("a (n p) d -> (a n) p d", p=P)[i - 2], P
            return io["x_sample"].rearrange("b t d -> (b t) d"), NS

        def norm_dst(i, hi, q):
            ks = slice(4 * q, 4 * q + 4)
            if i < 2:
                return (memTh if hi else memTl)[:, ks, P * i:P * i + P]
            n = P if i < 10 else NS
            return (hTh if hi else hTl)[:, ks, P * (i - 2):P * (i - 2) + n]

        def keys(a):
            u = units[a]
            if u[0] == "mem":
                return 2, None, 0
            _, g, b, _ = u
            if g == 2:
                return 1, "two", b
            if b == 0 or (g == 1 and b % 2 == 0):
                return 1, "diag", b
            return 2, "prev", b - 1

        last_of_chunk = {}
        for s in sched:
            if s in proj:
                last_of_chunk[s[1]] = s
        chunk_end = {n: proj[s] + 1 for n, s in last_of_chunk.items()}
        n_norm = 11
        norms_before, turns_before, nn, nt = {}, {}, 0, 0
        for s in sched:
            norms_before[s], turns_before[s] = nn, nt
            nn += s[0] == "norm_b"
            nt += s[0] == "turn"
        v_stores_before, v_stores_total = {}, 0
        for s in sched:
            if s[0] != "tok":
                continue
            kind, detail = chunks[s[1]][0], chunks[s[1]][1]
            if kind == "mv":
                v_stores_total += 1
            elif kind == "v" and s[2] < NB:
                v_stores_before.setdefault(detail[0], v_stores_total)
                v_stores_total += len(kv_rows(detail[0], s[2], 1, 0, CW))
        o_stores_before = [[0, 0]]
        for o in range(o_count):
            a = max(a for a in o_use if o_use[a] == o)
            row = list(o_stores_before[-1])
            row[o % 2] += 1
            o_stores_before.append(row)

        s_dD = sem("s_dD")
        s_dL = sem("s_dL")
        s_dM = sem("s_dM")
        s_db = sem("s_db")
        s_dbt = sem("s_dbt")
        s_dcb = sem("s_dcb")
        s_ddf = sem("s_ddf")
        s_do = sem("s_do")
        s_ds = sem("s_ds")
        s_dsn = sem("s_dsn")
        s_dt = sem("s_dt")
        s_dxd = sem("s_dxd")
        s_dxt = sem("s_dxt")
        s_dy = sem("s_dy")
        s_dyd = sem("s_dyd")
        s_dyp = sem("s_dyp")
        s_dys = sem("s_dys")
        s_eb = sem("s_eb")
        s_ec = sem("s_ec")
        s_ecm = sem("s_ecm")
        s_eld = [sem(f"s_eld{i}") for i in range(2)]
        s_en = sem("s_en")
        s_eo = sem("s_eo")
        s_es = sem("s_es")
        s_est = sem("s_est")
        s_et = sem("s_et")
        s_fs = sem("s_fs")
        s_fst8 = sem("s_fst8")
        s_ft = sem("s_ft")
        s_g1 = sem("s_g1")
        s_kv = [sem(f"s_kv{i}") for i in range(6)]
        s_m = sem("s_m")
        s_mgd = sem("s_mgd")
        s_mge = sem("s_mge")
        s_mgl = [sem(f"s_mgl{i}") for i in range(2)]
        s_mgm = sem("s_mgm")
        s_mgs = [sem(f"s_mgs{i}") for i in range(2)]
        s_mgt = sem("s_mgt")
        s_mgx = sem("s_mgx")
        s_mh = sem("s_mh")
        s_ml = sem("s_ml")
        s_nf = sem("s_nf")
        s_p1 = sem("s_p1")
        s_p1st = sem("s_p1st")
        s_pjv = sem("s_pjv")
        s_s0 = sem("s_s0")
        s_s0a = sem("s_s0a")
        s_s0p = sem("s_s0p")
        s_sa = sem("s_sa")
        s_sb1 = sem("s_sb1")
        s_sb2 = sem("s_sb2")
        s_sc5 = sem("s_sc5")
        s_sc6 = sem("s_sc6")
        s_skA = sem("s_skA")
        s_skD = sem("s_skD")
        s_sks = sem("s_sks")
        s_skt = sem("s_skt")
        s_sm = sem("s_sm")
        s_sn = sem("s_sn")
        s_snc = sem("s_snc")
        s_snp = sem("s_snp")
        s_so = sem("s_so")
        s_sost = sem("s_sost")
        s_sp = sem("s_sp")
        s_spz = sem("s_spz")
        s_sqc = sem("s_sqc")
        s_sqt = sem("s_sqt")
        s_sv = sem("s_sv")
        s_sw = sem("s_sw")
        s_sx = sem("s_sx")
        s_szt = sem("s_szt")
        s_tl = sem("s_tl")
        s_tle = sem("s_tle")
        s_tls = sem("s_tls")
        s_tlt = sem("s_tlt")
        s_xc = sem("s_xc")
        s_xr = [sem(f"s_xr{i}") for i in range(4)]
        s_y = sem("s_y")
        s_yah = sem("s_yah")
        s_yal = sem("s_yal")
        s_yald = [sem(f"s_yald{i}") for i in range(4)]
        s_yst = [sem(f"s_yst{i}") for i in range(2)]

        xflat = xc[:, :, :].rearrange("p f n -> p (f n)")
        xcs = xflat[:, 0:16 * NS].rearrange("p (f n) -> p f n", f=16)
        Lflat = Lm[:, :, :].rearrange("p h n -> p (h n)")
        cmask = gate1[:, 0, 0:D].rearrange("p (g b n) -> p g b n", g=SG, b=BS)
        tails = acc1[:, 128:128 + 16 * 35].rearrange("p (f n) -> p f n", f=16)
        cdraw, cdcol = sc[:, 7, 0:64], sc[:, 8, 0:64]
        out_no = {}
        for s in sched:
            if s[0] == "out":
                out_no[s] = len(out_no)
        first_p2 = min(u for s, u in proj.items() if s[0] == "p2") - n_act_proj
        first_out = min(u for s, u in proj.items() if s[0] == "out") - n_act_proj

        def prev_slot(b):
            return yst[:, :, :] if b % 2 == 0 else xflat[:, D:2 * D].rearrange("p (i n) -> p i n", i=8)

        def btb(b):
            return yraw[0:NS, 512 * (b % 2):512 * (b % 2) + 512]

        def ya_slot(k):
            return (yraw[:, :], acc1[:, :], gate1[:, 0, :], gate1[:, 1, :])[k % 4]

        def yb_slot(k):
            return (yraw2, gate2, acc2)[k % 3][:, :]

        def yst_of(c):
            return yst if c < NB else yst2

        def Lm_of(c, q):
            if c < NB:
                return Lm[:, 4 * q:4 * q + 4, :]
            return Lflat[0:NS, P * q:P * q + P].rearrange("p (h n) -> p h n", h=4)

        def D_of(c, q):
            m = P if c < NB else NS
            return bank[3 + q % 2][0:m, 0:4 * m].rearrange("p (h n) -> p h n", h=4)

        def wait_part1_stores(eng):
            eng.wait_ge(s_vst, 16 * v_stores_total)
            for i in range(4):
                eng.wait_ge(s_row[i], 16 * stored_before[-1][i])
            for i in range(2):
                eng.wait_ge(s_fst[i], 16 * ((len(feat_no) - i + 1) // 2))
                eng.wait_ge(s_ost[i], 16 * o_stores_before[-1][i])
            eng.wait_ge(s_tail, 16 * 32)

        def merge_free(eng):
            eng.wait_ge(s_pv, len(units))

        def late_free(eng):
            eng.wait_ge(s_sost, 32)
            eng.wait_ge(s_pj, n_act_proj)
            eng.wait_ge(s_sv, len(sets))

        def last_free(eng):
            eng.wait_ge(s_tls, 16 * 9)
            eng.wait_ge(s_est, 16 * BS)

        block = ctx.enter_context(nc.Block())

        @block.sync
        def _(sp):
            sp.dma_start(con[:, :], io["const"]).then_inc(s_const, 16)
            sp.dma_start(normw[:, 0, :], io["mem_norm_w"].partition_broadcast(P)).then_inc(s_const, 16)
            sp.dma_start(normw[:, 1, :], io["norm_in_w"].partition_broadcast(P)).then_inc(s_const, 16)
            loaded = 0
            for s in sched:
                if s[0] == "norm_a":
                    i = s[1]
                    if i >= 2:
                        sp.wait_ge(s_xt, i - 1)
                    src, n = norm_src(i)
                    sp.dma_start(xin[0:n, i % 2, :], src).then_inc(s_x[i % 2], 16)
                    if i == 1:
                        sp.dma_start(wdt_raw[:, :, :], io["w_in"][:, C_DT:C_DT + SH].rearrange("(k p) n -> p k n", p=P)).then_inc(s_wdt, 16)
                elif s[0] in ("split0", "split"):
                    n = s[1] if s[0] == "split0" else s[1] + 2
                    if n >= n_chunks:
                        continue
                    if n >= 1:
                        sp.wait_ge(s_wlo, n)
                    for i, src in enumerate(wsrc(n)):
                        sp.dma_start(w_raw[:, 4 * i:4 * i + 4, :], src).then_inc(s_w, 16)
                elif s[0] == "softmax" and units[s[1]][0] == "mem":
                    t = units[s[1]][1]
                    if t == 0:
                        k = max(feat_no[k] for k in feat_no if chunks[k[0]][1] >= FT_QMEM)
                        for j in range(2):
                            sp.wait_ge(s_fst[j], 16 * ((k - j) // 2 + 1))
                    for x in ((0, 1) if t == 0 else (t + 1,)):
                        if x >= NB:
                            continue
                        if x >= 2:
                            sp.wait_ge(s_sc, x - 1)
                            sp.wait_ge(s_o, x - 1)
                        for buf, ft in ((qmem, FT_QMEM), (zmem, FT_ZMEM)):
                            sp.dma_start(buf[:, x % 2, :, :], featT[ft:ft + 4, :, P * x:P * x + P].rearrange("h p n -> p h n")).then_inc(s_qm[x % 2], 16)
                elif s[0] == "merge":
                    b = s[1]
                    if b == 0:
                        wait_part1_stores(sp)
                        sp.wait_ge(s_pv, len(units))
                    if b >= 2:
                        sp.wait_ge(s_mgd, b - 1)
                    for g in range(NG):
                        sp.dma_start(mo[:, b % 2, g, :], orow[g][P * b:P * b + P]).then_inc(s_mgl[b % 2], 16)
                    sp.dma_start(mz[:, b % 2, :], zarow[P * b:P * b + P]).then_inc(s_mgl[b % 2], 16)
                elif s[0] == "sprep":
                    g = s[1]
                    if g == 0:
                        sp.wait_ge(s_mgt, NB)
                        sp.wait_ge(s_mgd, NB)
                        for i in range(2):
                            sp.wait_ge(s_mgs[i], 16 * 4)
                        for h in range(MH):
                            sp.dma_start(mq[:, h, :], featT[FT_QMEM + h, :, SEQ:]).then_inc(s_spz, 16)
                            sp.dma_start(mzs[:, h, :], featT[FT_ZMEM + h, :, SEQ:]).then_inc(s_spz, 16)
                        sp.dma_start(zas[0:NS, :], zarow[SEQ:]).then_inc(s_spz, 16)
                    else:
                        sp.wait_ge(s_sqt, g)
                    src = qkv_s[:, 3 * AW * g:3 * AW * g + 3 * AW].rearrange("n (j c) -> n j c", j=3)
                    sp.dma_start(qkS[:, :, :], src[:, 0:2, :]).then_inc(s_sp, 16)
                    sp.dma_start(vS[:, g, :], src[:, 2, :]).then_inc(s_sp, 16)
                elif s[0] in ("skey", "sval") and s[1] < len(sets):
                    q = s[1] + (len(sets) if s[0] == "sval" else 0)
                    kv = int(s[0] == "sval")
                    kind, b, g, t = sets[s[1]]
                    if q >= NRING:
                        free = q - NRING + 1
                        if free <= len(sets):
                            sp.wait_ge(s_skt, free)
                        else:
                            sp.wait_ge(s_sv, free - len(sets))
                    if kind == "mem":
                        src = io["cache_mem_kv"][b, P * g:P * g + P, kv].rearrange("n h d -> n (h d)")
                    else:
                        cache = io[("cache_win128_kv", "cache_win512_kv", "cache_win2048_kv")[g]][b]
                        if g:
                            cache = cache.rearrange("(n r) s h d -> r n s h d", r=GROUPS[g][1])[t]
                        src = cache[:, kv].rearrange("n h d -> n (h d)")
                    sp.dma_start(kvring[:, q % NRING, :], src).then_inc(s_kv[q % NRING], 16)
                elif s[0] == "ssd_setup":
                    late_free(sp)
                    sp.dma_start(ssdw[:, :], io["ssd_norm_w"].partition_broadcast(P)).then_inc(s_sw, 16)
                elif s[0] == "ya":
                    k = s[1]
                    if k >= 4:
                        sp.wait_ge(s_yal, k - 3)
                    sp.dma_start(ya_slot(k), yT[8 + k]).then_inc(s_yald[k % 4], 16)
                elif s[0] == "yb":
                    k = s[1]
                    if k == 0:
                        last_free(sp)
                        for i in range(2):
                            sp.wait_ge(s_yst[i], 16 * (5 - i))
                    if k >= 3:
                        sp.wait_ge(s_yal, KT8 + k - 2)
                    sp.dma_start(yb_slot(k), yT[k]).then_inc(s_yald[k % 3], 16)
                elif s[0] == "p1" and s[3] == 0 and s[4] == 0:
                    ft = chunks[s[1]][1] + s[2]
                    if ft == 0:
                        sp.wait_ge(s_yal, KT8)
                    else:
                        sp.wait_ge(s_p1, ft)
                    for i in range(2):
                        sp.dma_start(gate1[:, i, :], featT[FT_GATE + 8 * (i + 1) + ft]).then_inc(s_g1, 16)
                elif s[0] == "p2" and s[3] == 0:
                    ft = chunks[s[1]][1] + s[2]
                    if ft == 0:
                        sp.wait_ge(s_yal, KT8 + KT8)
                        sp.wait_ge(s_p1st, 16 * KT8)
                    else:
                        sp.wait_ge(s_m, 3 * ft)
                    sp.dma_start(gate2[:, :], featT[FT_GATE + ft]).then_inc(s_g1, 16)
                    sp.dma_start(acc2[:, :], accT[ft]).then_inc(s_g1, 16)
                elif s[0] == "ssd" and s[2] == 0:
                    c = s[1]
                    if c >= 1:
                        sp.wait_ge(s_do, c)
                        sp.wait_ge(s_dyd, c)
                    if c < NB:
                        sp.dma_start(xc[:, :, :], featT[0:16, :, P * c:P * c + P].rearrange("f p n -> p f n")).then_inc(s_xc, 16)
                        sp.dma_start(zt[:, :], zrow[P * c:P * c + P]).then_inc(s_xc, 16)
                    else:
                        sp.dma_start(xcs, featT[0:16, :, SEQ:].rearrange("f p n -> p f n")).then_inc(s_xc, 16)
                        sp.dma_start(zt[0:NS, :], zrow[SEQ:]).then_inc(s_xc, 16)
                elif s[0] == "ssd_sb":
                    b = s[1]
                    if b == 0:
                        for i in range(2):
                            sp.wait_ge(s_yst[i], 16 * 4)
                    if b >= 2:
                        sp.wait_ge(s_en, b - 1)
                    sp.dma_start(prev_slot(b), io["state_ssm"][b].rearrange("h p n -> (h p) n").rearrange("(i q) n -> q i n", q=P)).then_inc(s_eld[b % 2], 16)
                elif s[0] == "tail":
                    sp.wait_ge(s_es, 8)
                    sp.wait_ge(s_en, 8)
                    sp.wait_ge(s_p1st, 16 * KT8)
                    sp.dma_start(tails, tailT.rearrange("f p n -> p f n")).then_inc(s_tl, 16)
                elif s[0] == "out":
                    _, n, t = s
                    x = out_no[s]
                    if x == 0:
                        sp.wait_ge(s_ml, 3 * KT8)
                        sp.dma_start(normf[:, :], io["norm_f_w"].partition_broadcast(P)).then_inc(s_nf, 16)
                    if x >= 4:
                        sp.wait_ge(s_pjv, first_out + x - 3)
                    c0 = CW * chunks[n][1]
                    m = P if t < NB else NS
                    src = io["x_prompt"][0, P * t:P * t + P, c0:c0 + CW] if t < NB else io["x_sample"].rearrange("b t d -> (b t) d")[:, c0:c0 + CW]
                    sp.dma_start(xres[0:m, x % 4, :], src).then_inc(s_xr[x % 4], 16)
        @block.gpsimd
        def _(pool):
            pool.dma_start(hrow[:, 0, :], io["dt_bias"].partition_broadcast(P)).then_inc(s_cv, 16)
            pool.dma_start(hrow[:, 1, :], io["a_log"].partition_broadcast(P)).then_inc(s_cv, 16)
            pool.dma_start(hrow[:, 2, :], io["d_skip"].partition_broadcast(P)).then_inc(s_cv, 16)
            pool.dma_start(obuf[0:64, 0, 0:P], io["conv_w"].rearrange("k (f p) -> (k f) p", p=P)).then_inc(s_cv, 16)
            pool.dma_start(obuf[64:80, 0, 0:P], io["conv_b"].rearrange("(f p) -> f p", p=P)).then_inc(s_cv, 16)
            for half in range(4):
                pool.dma_start(softT[0:24, half // 2, 2 * (half % 2):2 * (half % 2) + 2, :, :].rearrange("p a b n -> p (a b n)"),
                               io["state_conv"].rearrange("b k c -> (b k) c")[:, 512 * half:512 * half + 512]).then_inc(s_cv, 16)
            for s in sched:
                if s[0] == "tok":
                    _, n, t = s
                    kind, detail = chunks[n][0], chunks[n][1]
                    u = proj[s]
                    if kind == "mv":
                        pool.wait_ge(s_pjev, u + 1)
                        pool.dma_start(outs[5].rearrange("a t s h d -> (a t) s (h d)")[P * t:P * t + P, 1, CW * detail:CW * detail + CW],
                                       Vm[:, t, CW * detail:CW * detail + CW]).then_inc(s_vst, 16)
                    elif kind == "v" and t < NB:
                        g, half = detail
                        pool.wait_ge(s_pjev, u + 1)
                        for p0, np_, dst in kv_rows(g, t, 1, CW * half, CW):
                            pool.dma_start(dst, V[p0:p0 + np_, t, CW * half:CW * half + CW]).then_inc(s_vst, 16)
                    else:
                        c = slot_of[s]
                        if not slot_stores[c]:
                            continue
                        if kind in ("q", "k"):
                            pool.wait_ge(s_rope, roped[s] + 1)
                        else:
                            pool.wait_ge(s_pjev, u + 1)
                        row = rows[:, c % 4, :]
                        st = s_row[c % 4]
                        if kind == "mk":
                            pool.dma_start(outs[5].rearrange("a t s h d -> (a t) s (h d)")[P * t:P * t + P, 0, CW * detail:CW * detail + CW], row).then_inc(st, 16)
                        elif kind in ("z", "za"):
                            dst = zrow if kind == "z" else zarow
                            m = P if t < NB else NS
                            pool.dma_start(dst[P * t:P * t + m, CW * detail:CW * detail + CW], row[0:m, :]).then_inc(st, 16)
                        elif t == NB:
                            g, half = detail
                            j = "qkv".index(kind)
                            c0 = (g * 3 + j) * AW + CW * half
                            pool.dma_start(qkv_s[:, c0:c0 + CW], row[0:NS, :]).then_inc(st, 16)
                            if j:
                                pool.dma_start(outs[8 + g].rearrange("b t s h d -> (b t) s (h d)")[:, j - 1, CW * half:CW * half + CW],
                                               row[0:NS, :]).then_inc(st, 16)
                        else:
                            g, half = detail
                            for p0, np_, dst in kv_rows(g, t, 0, CW * half, CW):
                                pool.dma_start(dst, row[p0:p0 + np_, :]).then_inc(st, 16)
                elif s[0] == "feat" and s[3] == 2:
                    k = feat_no[(s[1], s[2])]
                    ft = chunks[s[1]][1] + s[2]
                    if is_conv[(s[1], s[2])]:
                        pool.wait_ge(s_silu, conv_no[(s[1], s[2])] + 1)
                        pool.dma_start(tailT[ft, :, 0:3], fraw[:, SEQ:SEQ + 3]).then_inc(s_tail, 16)
                        pool.dma_start(tailT[ft, :, 3:35].rearrange("p (b t) -> p b t", t=TS),
                                       fraw[:, 3 + SEQ:].rearrange("p (b t) -> p b t", t=TS + 3)[:, :, 3:]).then_inc(s_tail, 16)
                    else:
                        pool.wait_ge(s_pjev, proj[s] + 1)
                    pool.dma_start(featT[ft], fstage[:, k % 2, :]).then_inc(s_fst[k % 2], 16)
                elif s[0] == "pv":
                    a = s[1]
                    u = units[a]
                    o = o_use[a]
                    if u[0] == "mem":
                        pool.wait_ge(s_o, o + 1)
                        pool.dma_start(yT[12:16, :, P * u[1]:P * u[1] + P].rearrange("h p n -> p h n"),
                                       obuf[:, o % 2, 0:512].rearrange("p (h n) -> p h n", h=MH)).then_inc(s_ost[o % 2], 16)
                    elif u[3] == 1:
                        pool.wait_ge(s_o, o + 1)
                        g, b = u[1], u[2]
                        if g == 0:
                            dsts = [(0, P, orow[g][P * b:P * b + P])]
                        elif g == 1:
                            dsts = [(0, P, orow[g].rearrange("(h i r) c -> h r i c", h=2, r=4)[b % 2, b // 2])]
                        else:
                            dsts = [(0, P, orow[g].rearrange("(i r) c -> r i c", r=8)[b])]
                        for p0, np_, dst in dsts:
                            pool.dma_start(dst, obuf[p0:p0 + np_, o % 2, :]).then_inc(s_ost[o % 2], 16)
                elif s[0] == "merge":
                    b = s[1]
                    pool.wait_ge(s_mge, b + 1)
                    pool.dma_start(yT[8:12, :, P * b:P * b + P].rearrange("i p n -> p i n"),
                                   mst[:, b % 2, :].rearrange("p (i n) -> p i n", i=4)).then_inc(s_mgs[b % 2], 16)
                elif s[0] == "sout":
                    wait_part1_stores(pool)
                    pool.wait_ge(s_so, 1)
                    for i in range(2):
                        pool.dma_start(yT[8 + 4 * i:12 + 4 * i, :, SEQ:].rearrange("h p n -> p h n"), ysam[:, i, :, :]).then_inc(s_sost, 16)
                elif s[0] == "p1" and s[3] == 1 and s[4] == 2:
                    ft = chunks[s[1]][1] + s[2]
                    pool.wait_ge(s_p1, ft + 1)
                    pool.dma_start(accT[ft], acc1[:, :]).then_inc(s_p1st, 16)
                elif s[0] == "ssd" and s[2] == 5:
                    c = s[1]
                    pool.wait_ge(s_dys, c + 1)
                    cols = slice(P * c, P * c + P) if c < NB else slice(SEQ, TOK)
                    m = P if c < NB else NS
                    pool.dma_start(yT[0:8, :, cols].rearrange("k p n -> p k n"), yst_of(c)[:, :, 0:m]).then_inc(s_yst[c % 2], 16)
                elif s[0] == "ssd_state":
                    pool.wait_ge(s_fs, 2)
                    pool.dma_start(outs[7].rearrange("a h p n -> (a h p) n").rearrange("(i q) n -> q i n", q=P),
                                   Lflat[:, 0:D].rearrange("p (i n) -> p i n", i=8)).then_inc(s_fst8, 16)
                elif s[0] == "ssd_sb":
                    b = s[1]
                    pool.wait_ge(s_en, b + 1)
                    pool.dma_start(outs[12][b].rearrange("h p n -> (h p) n").rearrange("(i q) n -> q i n", q=P),
                                   Lflat[:, D:2 * D].rearrange("p (i n) -> p i n", i=8)).then_inc(s_est, 16)
                elif s[0] == "tail":
                    pool.wait_ge(s_tle, 4)
                    pool.dma_start(outs[6][0], Lflat[0:3, :]).then_inc(s_tls, 16)
                    for b in range(BS):
                        pool.dma_start(outs[11][b], Lflat[4 + 4 * b:7 + 4 * b, :]).then_inc(s_tls, 16)
                elif s[0] == "out" and chunks[s[1]][1] == 3:
                    t = s[2]
                    pool.wait_ge(s_xn, n_norm + NB + 1 + t + 1)
                    if t < NB:
                        pool.dma_start(outs[0][0, P * t:P * t + P], orows[:, t, :]).then_inc(s_y, 16)
                    else:
                        pool.dma_start(outs[1].rearrange("b t d -> (b t) d"), orows[0:NS, t, :]).then_inc(s_y, 16)
            pool.wait_ge(s_tls, 16 * 9)
            pool.wait_ge(s_est, 16 * BS)
            pool.wait_ge(s_fst8, 16)
            pool.wait_ge(s_p1st, 16 * KT8)
            pool.wait_ge(s_y, 16 * (NB + 1))

        @block.scalar
        def _(act):
            nchain = [0]

            def link(ins):
                nchain[0] += 1
                ins.then_inc(s_act, 1)
                act.wait_ge(s_act, nchain[0])

            def split_hi(n):
                act.wait_ge(s_w, 32 * (n + 1))
                if n >= 2:
                    act.wait_ge(s_pj, chunk_end[n - 2])
                act.activation(w_hi[:, n % 2, :, :], w_raw[:, :, :], ACT.Copy).then_inc(s_whi, 1)

            for s in sched:
                if s[0] == "norm_a":
                    i = s[1]
                    m = P if i < 10 else NS
                    act.wait_ge(s_x[i % 2], 16 * (i // 2 + 1))
                    if i >= 1:
                        act.wait_ge(s_sq, i)
                    act.activation(xsq[0:m, :], xin[0:m, i % 2, :], ACT.Square, accum_out=small[0:m, i:i + 1]).then_inc(s_sq, 1)
                    act.wait_ge(s_var, i + 1)
                    act.activation(small[0:m, i:i + 1], small[0:m, i:i + 1], ACT.Sqrt).then_inc(s_rstd, 1)
                elif s[0] == "norm_b":
                    i = s[1]
                    m = P if i < 10 else NS
                    act.wait_ge(s_xt, i + 1)
                    for q in range(2):
                        src = bank[3 + 2 * (i % 2) + q][:, :].rearrange("p (k n) -> p k n", k=4)[:, :, 0:m]
                        act.activation(norm_dst(i, True, q), src, ACT.Copy).then_inc(s_hhi, 1)
                elif s[0] in ("split0", "split"):
                    n = s[1] if s[0] == "split0" else s[1] + 2
                    if n < n_chunks:
                        split_hi(n)
                elif s[0] == "dt":
                    act.wait_ge(s_wdt, 16)
                    act.activation(wdt_hi[:, :, :], wdt_raw[:, :, :], ACT.Copy).then_inc(s_wdth, 1)
                    act.wait_ge(s_dtp, 1)
                    act.wait_ge(s_dve, 2)
                    act.activation(dtv[:, 0:P], bank[3][:, 0:P], ACT.Copy)
                    act.activation(dtv[0:NS, P:], bank[3][0:NS, P:P + SH], ACT.Copy).then_inc(s_dte, 1)
                elif s[0] == "tok":
                    _, n, t = s
                    kind, detail = chunks[n][0], chunks[n][1]
                    u = proj[s]
                    m = P if t < NB else NS
                    psum = bank[u % 3][0:m, 0:CW]
                    func = ACT.Silu if kind in ("z", "za") else ACT.Copy
                    if kind == "mv":
                        dst = Vm[:, t, CW * detail:CW * detail + CW]
                    elif kind == "v" and t < NB:
                        g, half = detail
                        dst = V[:, t, CW * half:CW * half + CW]
                        if t == 0 and half == 0:
                            act.wait_ge(s_pv, first_att[g])
                            act.wait_ge(s_vst, 16 * v_stores_before[g])
                    else:
                        c = slot_of[s]
                        dst = rows[0:m, c % 4, :]
                        if c >= 4:
                            if c - 4 in turn_of_slot:
                                act.wait_ge(s_turn, turn_of_slot[c - 4] + 1)
                            if stored_before[c][c % 4]:
                                act.wait_ge(s_row[c % 4], 16 * stored_before[c][c % 4])
                    act.wait_ge(s_pj, u + 1)
                    act.activation(dst, psum, func).then_inc(s_pjev, 1)
                elif s[0] == "feat":
                    _, n, f, j = s
                    u = proj[s]
                    k = feat_no[(n, f)]
                    ft = chunks[n][1] + f
                    psum = bank[u % 3][:, 0:THIRD]
                    conv = is_conv[(n, f)]
                    if j == 0:
                        if conv:
                            c = conv_no[(n, f)]
                            if c >= 1:
                                act.wait_ge(s_conv, c)
                                act.wait_ge(s_tail, 32 * c)
                        elif k >= 2:
                            act.wait_ge(s_fst[k % 2], feat_done_stores(k))
                    act.wait_ge(s_pj, u + 1)
                    if conv:
                        if j < 2:
                            act.activation(fraw[:, 3 + THIRD * j:3 + THIRD * j + THIRD], psum, ACT.Copy).then_inc(s_pjev, 1)
                        else:
                            k0 = SEQ - 2 * THIRD
                            act.activation(fraw[:, 3 + 2 * THIRD:3 + SEQ], psum[:, 0:k0], ACT.Copy)
                            act.activation(fraw[:, 3 + SEQ:].rearrange("p (b t) -> p b t", t=TS + 3)[:, :, 3:],
                                           psum[:, k0:].rearrange("p (b t) -> p b t", t=TS), ACT.Copy).then_inc(s_pjev, 1)
                            act.wait_ge(s_conv, conv_no[(n, f)] + 1)
                            act.activation(fstage[:, k % 2, :], fstage[:, k % 2, :], ACT.Silu).then_inc(s_silu, 1)
                    else:
                        func = ACT.Sigmoid if ft < FT_QMEM else (ACT.Copy if ft < FT_ZMEM else ACT.Silu)
                        act.activation(fstage[:, k % 2, THIRD * j:THIRD * j + THIRD], psum, func).then_inc(s_pjev, 1)
                elif s[0] == "softmax":
                    a = s[1]
                    u = units[a]
                    w = keys(a)[0] * P
                    act.wait_ge(s_max, a + 1)
                    o = o_use[a]
                    for h in range(4):
                        if u[0] == "mem":
                            scale, total = MD ** -0.5, mstat[:, a % 2, h:h + 1]
                        else:
                            scale = HD ** -0.5
                            total = obuf[:, o % 2, AW + HEADS + 4 * u[3] + h:AW + HEADS + 4 * u[3] + h + 1]
                        ins = act.activation(soft[:, a % 2, h, 0:w], soft[:, a % 2, h, 0:w], ACT.Exp,
                                             bias=nmax[:, a % 2, h:h + 1], scale=scale, accum_out=total)
                    ins.then_inc(s_exp, 1)
                elif s[0] == "ptrans":
                    a = s[1]
                    act.wait_ge(s_pt, a + 1)
                    if a >= 2:
                        act.wait_ge(s_pv, a - 1)
                    kb = keys(a)[0]
                    act.activation(softT[:, a % 2, 0:2, 0:kb, :],
                                   bank[5][:, 0:2 * kb * P].rearrange("p (h k n) -> p h k n", h=2, k=kb), ACT.Copy).then_inc(s_ptA, 1)
                elif s[0] == "merge":
                    b = s[1]
                    act.wait_ge(s_mgm, b + 1)
                    act.activation(mw[:, 32:56], mw[:, 0:24], ACT.Exp, scale=HD ** -0.5).then_inc(s_mgx, 1)
                    act.wait_ge(s_mgt, b + 1)
                    if b >= 2:
                        act.wait_ge(s_mgs[b % 2], 16 * (b // 2))
                    act.activation(mst[:, b % 2, :], bank[3 + b % 2][:, :], ACT.Copy).then_inc(s_mge, 1)
                elif s[0] == "sprep":
                    g = s[1]
                    act.wait_ge(s_snp, g + 1)
                    act.activation(sTn[:, g, :], bank[7][0:NS, 0:256], ACT.Copy).then_inc(s_snc, 1)
                elif s[0] == "skey" and s[1] < len(sets) and s[1] % 2 == 0:
                    n = s[1]
                    act.wait_ge(s_skt, n + 1)
                    if n >= 2:
                        act.wait_ge(s_sks, n - 1)
                    act.activation(kset[:, 0, :, :], bank[5][:, :].rearrange("p (i n) -> p i n", i=4), ACT.Copy).then_inc(s_skA, 1)
                elif s == ("ssoft", "att"):
                    act.wait_ge(s_sks, len(sets))
                    act.activation(sT[:, 0:2, :], bank[3][:, :].rearrange("p (g n) -> p g n", g=2), ACT.Copy)
                    act.activation(sT[:, 2, :], bank[4][:, 0:256], ACT.Copy)
                    act.activation(mS, bank[7][:, 0:256], ACT.Copy).then_inc(s_sa, 1)
                    for half in range(2):
                        act.wait_ge(s_sm, half + 1)
                        row = srow[:, half, :, :].rearrange("p g n -> p (g n)")
                        act.activation(row, row, ACT.Exp, bias=sstat[:, 2 + half:3 + half], scale=HD ** -0.5,
                                       accum_out=sstat[:, 4 + half:5 + half]).then_inc(s_sx, 1)
                        act.wait_ge(s_sb2, half + 1)
                        act.activation(pT[:, :, half, :], bank[5][:, 0:384].rearrange("p (g n) -> p g n", g=NG), ACT.Copy).then_inc(s_sc5, 1)
                elif s == ("ssoft", "mem"):
                    act.wait_ge(s_sm, 3)
                    act.activation(mrow, mrow, ACT.Exp, bias=sstat[:, 9:10], scale=MD ** -0.5,
                                   accum_out=sstat[:, 10:11]).then_inc(s_sx, 1)
                elif s[0] == "ssd_setup":
                    late_free(act)
                    act.wait_ge(s_cv, 16 * 9)
                    act.activation(hrow[:, 1, :], hrow[:, 1, :], ACT.Exp).then_inc(s_s0a, 1)
                    act.wait_ge(s_s0, 1)
                    act.activation(sc[:, 9, :], sc[:, 7, :], ACT.Exp, scale=-1.0).then_inc(s_s0a, 1)
                    act.wait_ge(s_s0, 2)
                    act.activation(sc[:, 4, :], sc[:, 7, :], ACT.Ln).then_inc(s_s0a, 1)
                    act.wait_ge(s_s0, 4)
                    for dst, src in ((3, 2), (4, 4), (5, 5)):
                        act.activation(sc[:, dst, 0:P], sc[:, src, 0:P], ACT.Exp)
                        act.activation(sc[0:NS, dst, P:], sc[0:NS, src, P:], ACT.Exp)
                    act.activation(cdcol, cdraw, ACT.Exp).then_inc(s_s0a, 1)
                elif s[0] == "ya":
                    k = s[1]
                    act.wait_ge(s_yald[k % 4], 16 * (k // 4 + 1))
                    act.activation(yAh[:, k, :], ya_slot(k), ACT.Copy).then_inc(s_yah, 1)
                elif s[0] == "yb":
                    k = s[1]
                    act.wait_ge(s_yald[k % 3], 32 + 16 * (k // 3 + 1))
                    act.activation(yBh[:, k, :], yb_slot(k), ACT.Copy).then_inc(s_yah, 1)
                elif s[0] == "ssd":
                    _, c, q = s
                    m = P if c < NB else NS
                    if q == 0:
                        act.wait_ge(s_dt, c + 1)
                        act.activation(xtok[0:m, 0:512], bank[3][0:m, :], ACT.Copy)
                        act.activation(xtok[0:m, 512:D], bank[4][0:m, :], ACT.Copy).then_inc(s_dxt, 1)
                        act.wait_ge(s_db, c + 1)
                        act.activation(btok[0:m, :], bank[5][0:m, :], ACT.Copy).then_inc(s_dbt, 1)
                    elif q in (1, 2):
                        for qq in (2 * q - 2, 2 * q - 1):
                            act.wait_ge(s_ddf, 4 * c + qq + 1)
                            l = Lm_of(c, qq)
                            act.activation(l, l, ACT.Exp).then_inc(s_dL, 1)
                    elif q == 5:
                        act.wait_ge(s_dyd, c + 1)
                        act.activation(yo[0:m, :], yy[0:m, :], ACT.Square, accum_out=small[0:m, 32 + c:33 + c]).then_inc(s_sq, 1)
                        act.wait_ge(s_var, n_norm + c + 1)
                        act.activation(small[0:m, 32 + c:33 + c], small[0:m, 32 + c:33 + c], ACT.Sqrt).then_inc(s_rstd, 1)
                        act.wait_ge(s_xt, n_norm + c + 1)
                        if c >= 1:
                            act.wait_ge(s_yst[(c - 1) % 2], 16 * ((c - 1) // 2 + 1))
                        for i in range(2):
                            ins = act.activation(yst_of(c)[:, 4 * i:4 * i + 4, 0:m],
                                                 bank[3 + i][:, :].rearrange("p (k n) -> p k n", k=4)[:, :, 0:m], ACT.Copy)
                        ins.then_inc(s_dys, 1)
                elif s[0] == "ssd_state":
                    act.wait_ge(s_ft, 1)
                    for i in range(2):
                        act.activation(Lflat[:, 512 * i:512 * i + 512], bank[3 + i][:, :], ACT.Copy).then_inc(s_fs, 1)
                elif s[0] == "ssd_sb":
                    b = s[1]
                    act.wait_ge(s_et, b + 1)
                    if b >= 1:
                        act.wait_ge(s_eo, b)
                    act.activation(state[:, 0:512], bank[3][:, :], ACT.Copy)
                    act.activation(state[:, 512:D], bank[4][:, :], ACT.Copy).then_inc(s_ec, 1)
                elif s[0] == "tail":
                    act.wait_ge(s_tlt, 1)
                    act.wait_ge(s_est, 16 * BS)
                    for i in range(4):
                        act.activation(Lflat[0:35, 512 * i:512 * i + 512], bank[3 + i][0:35, :], ACT.Copy).then_inc(s_tle, 1)
                elif s[0] == "p2":
                    _, n, f, j = s
                    ft = chunks[n][1] + f
                    x = 3 * ft + j
                    act.wait_ge(s_m, x + 1)
                    act.activation(mTh[:, ft, THIRD * j:THIRD * j + THIRD], yraw2[:, THIRD * j:THIRD * j + THIRD], ACT.Copy).then_inc(s_mh, 1)
                elif s[0] == "out" and chunks[s[1]][1] == 3:
                    t = s[2]
                    m = P if t < NB else NS
                    act.wait_ge(s_pjv, first_out + out_no[s] + 1)
                    if t:
                        act.wait_ge(s_sq, n_norm + NB + 1 + t)
                    act.activation(osq[0:m, :], orows[0:m, t, :], ACT.Square, accum_out=small[0:m, 44 + t:45 + t]).then_inc(s_sq, 1)
                    act.wait_ge(s_var, n_norm + NB + 1 + t + 1)
                    act.activation(small[0:m, 44 + t:45 + t], small[0:m, 44 + t:45 + t], ACT.Sqrt).then_inc(s_rstd, 1)

        @block.vector
        def _(dve):
            nchain = [0]

            def link(ins):
                nchain[0] += 1
                ins.then_inc(s_dve, 1)
                dve.wait_ge(s_dve, nchain[0])

            def split_lo(n):
                dve.wait_ge(s_whi, n + 1)
                dve.tensor_tensor(w_lo[:, n % 2, :, :], w_raw[:, :, :], w_hi[:, n % 2, :, :].bitcast(F32),
                                  ALU.subtract).then_inc(s_wlo, 1)

            link(dve.memset(fraw[:, 0:3], 0.0))
            link(dve.memset(dtv[:, P:], 0.0))
            dve.wait_ge(s_const, 48)
            for s in sched:
                if s[0] == "norm_a":
                    i = s[1]
                    m = P if i < 10 else NS
                    r = small[0:m, i:i + 1]
                    dve.wait_ge(s_sq, i + 1)
                    link(dve.tensor_scalar(r, r, 1.0 / D, EPS, ALU.mult, ALU.add))
                    dve.reciprocal(r, r).then_inc(s_var, 1)
                    dve.wait_ge(s_rstd, i + 1)
                    x = xin[0:m, i % 2, :]
                    dve.scalar_tensor_tensor(x, x, r, normw[0:m, 0 if i < 2 else 1, :], ALU.mult, ALU.mult).then_inc(s_xn, 1)
                elif s[0] == "norm_b":
                    i = s[1]
                    m = P if i < 10 else NS
                    for q in range(2):
                        dve.wait_ge(s_hhi, 2 * i + q + 1)
                        src = bank[3 + 2 * (i % 2) + q][:, :].rearrange("p (k n) -> p k n", k=4)[:, :, 0:m]
                        dve.tensor_tensor(norm_dst(i, False, q), src, norm_dst(i, True, q).bitcast(F32), ALU.subtract).then_inc(s_hlo, 1)
                elif s[0] in ("split0", "split"):
                    n = s[1] if s[0] == "split0" else s[1] + 2
                    if n < n_chunks:
                        split_lo(n)
                elif s[0] == "dt":
                    dve.wait_ge(s_wdth, 1)
                    dve.tensor_tensor(wdt_lo[:, :, :], wdt_raw[:, :, :], wdt_hi[:, :, :].bitcast(F32), ALU.subtract).then_inc(s_wdtl, 1)
                    dve.wait_ge(s_cvt, 1)
                    dve.tensor_copy(convw[:, :], bank[7][:, 0:80]).then_inc(s_cvc, 1)
                    dve.wait_ge(s_cvt, 2)
                    dve.tensor_copy(cstate[:, :, :], bank[4][:, 0:384].rearrange("p (f b) -> p f b", b=24)).then_inc(s_cvc, 1)
                elif s[0] == "tok" and chunks[s[1]][0] in ("q", "k"):
                    _, n, t = s
                    g, half = chunks[n][1]
                    m = P if t < NB else NS
                    c = slot_of[s]
                    x = rows[0:m, c % 4, :].rearrange("p (h d) -> p h d", d=HD)
                    at = 3 * NB if t == NB else g * NB + t
                    cc = table("rope")[0:m, 32 * at:32 * at + 16].unsqueeze(1).broadcast_to([m, 4, 16])
                    ss = table("rope")[0:m, 32 * at + 16:32 * at + 32].unsqueeze(1).broadcast_to([m, 4, 16])
                    tmp = small[0:m, 0:64].rearrange("p (h d) -> p h d", h=4)
                    dve.wait_ge(s_pjev, proj[s] + 1)
                    if roped[s]:
                        dve.wait_ge(s_rope, roped[s])
                    dve.tensor_tensor(tmp[:, :, 0:8], x[:, :, 8:16], ss[:, :, 0:8], ALU.mult)
                    link(dve.tensor_tensor(tmp[:, :, 8:16], x[:, :, 0:8], ss[:, :, 8:16], ALU.mult))
                    link(dve.tensor_tensor(x[:, :, 0:16], x[:, :, 0:16], cc, ALU.mult))
                    dve.tensor_tensor(x[:, :, 0:16], x[:, :, 0:16], tmp, ALU.add).then_inc(s_rope, 1)
                elif s[0] == "turn":
                    _, n, t = s
                    v = turned[s]
                    kind, detail = chunks[n][0], chunks[n][1]
                    src = bank[5 + v % 2][:, 0:CW].rearrange("p (i n) -> p i n", i=2)
                    if kind == "mk":
                        dst = KmT[:, 2 * detail:2 * detail + 2, P * t:P * t + P]
                    else:
                        g, half = detail
                        if t == 0 and half == 0:
                            dve.wait_ge(s_pv, first_att[g])
                        dst = (QT if kind == "q" else KTt)[:, 2 * half:2 * half + 2, P * t:P * t + P]
                    dve.wait_ge(s_turn, v + 1)
                    dve.tensor_copy(dst, src).then_inc(s_turned, 1)
                elif s[0] == "feat" and s[3] == 2 and is_conv[(s[1], s[2])]:
                    k = feat_no[(s[1], s[2])]
                    ft = chunks[s[1]][1] + s[2]
                    dve.wait_ge(s_pjev, proj[s] + 1)
                    if k >= 2:
                        dve.wait_ge(s_fst[k % 2], feat_done_stores(k))
                    raw_s = fraw[:, 3 + SEQ:].rearrange("p (b t) -> p b t", t=TS + 3)
                    link(dve.tensor_copy(raw_s[:, :, 0:3], cstate[:, ft, :].rearrange("p (b t) -> p b t", t=3)))
                    y = fstage[:, k % 2, 0:SEQ]
                    ys = fstage[:, k % 2, SEQ:TOK].rearrange("p (b t) -> p b t", t=TS)
                    for tap in range(CONV):
                        wcol = convw[:, 16 * tap + ft:16 * tap + ft + 1]
                        x, xs = fraw[:, tap:tap + SEQ], raw_s[:, :, tap:tap + TS]
                        if tap == 0:
                            bcol = convw[:, 64 + ft:65 + ft]
                            dve.tensor_scalar(y, x, wcol, bcol, ALU.mult, ALU.add)
                            link(dve.tensor_scalar(ys, xs, wcol, bcol, ALU.mult, ALU.add))
                        elif tap < CONV - 1:
                            dve.scalar_tensor_tensor(y, x, wcol, y, ALU.mult, ALU.add)
                            link(dve.scalar_tensor_tensor(ys, xs, wcol, ys, ALU.mult, ALU.add))
                        else:
                            dve.scalar_tensor_tensor(y, x, wcol, y, ALU.mult, ALU.add)
                            dve.scalar_tensor_tensor(ys, xs, wcol, ys, ALU.mult, ALU.add).then_inc(s_conv, 1)
                elif s[0] == "softmax":
                    a = s[1]
                    u = units[a]
                    kb, mask, _ = keys(a)
                    w = kb * P
                    slot = a % 2
                    o = o_use[a]
                    dve.wait_ge(s_sc, a + 1)
                    if a >= 2:
                        dve.wait_ge(s_pt, a - 1)
                    for j in range(2):
                        src = bank[3 + j][:, :].rearrange("p (h n) -> p h n", h=2)[:, :, 0:w]
                        dst = soft[:, slot, j::2, 0:w]
                        if mask is None:
                            ins = dve.tensor_copy(dst, src)
                        else:
                            c0 = CONST_AT[mask][0]
                            ins = dve.tensor_tensor(dst, src, con[:, c0:c0 + w].unsqueeze(1).broadcast_to([P, 2, w]), ALU.add)
                    ins.then_inc(s_msk, 1)
                    dve.wait_ge(s_msk, a + 1)
                    if u[0] == "mem":
                        top = mstat[:, slot, 4:8]
                        scale = MD ** -0.5
                    else:
                        if u[3] == 0 and o >= 2:
                            dve.wait_ge(s_ost[o % 2], 16 * o_stores_before[o][o % 2])
                        top = obuf[:, o % 2, AW + 4 * u[3]:AW + 4 * u[3] + 4]
                        scale = HD ** -0.5
                    link(dve.tensor_reduce(top, soft[:, slot, :, 0:w], AX, ALU.max))
                    if a >= 2:
                        dve.wait_ge(s_exp, a - 1)
                    dve.tensor_scalar(nmax[:, slot, :], top, -scale, None, ALU.mult).then_inc(s_max, 1)
                    if u[0] == "mem":
                        dve.wait_ge(s_exp, a + 1)
                        link(dve.reciprocal(mstat[:, slot, 8:12], mstat[:, slot, 0:4]))
                        dve.tensor_tensor(soft[:, slot, :, :], soft[:, slot, :, :],
                                          mstat[:, slot, 8:12].unsqueeze(2).broadcast_to([P, 4, CW]), ALU.mult).then_inc(s_pn, 1)
                elif s[0] == "ptrans":
                    a = s[1]
                    kb = keys(a)[0]
                    dve.wait_ge(s_pt, a + 1)
                    if a >= 2:
                        dve.wait_ge(s_pv, a - 1)
                    dve.tensor_copy(softT[:, a % 2, 2:4, 0:kb, :],
                                    bank[6][:, 0:2 * kb * P].rearrange("p (h k n) -> p h k n", h=2, k=kb)).then_inc(s_ptD, 1)
                elif s[0] == "pv":
                    a = s[1]
                    u = units[a]
                    o = o_use[a]
                    if u[0] == "mem":
                        dve.wait_ge(s_pv, a + 1)
                        if o >= 2:
                            dve.wait_ge(s_ost[o % 2], 16 * o_stores_before[o][o % 2])
                        dve.wait_ge(s_qm[o % 2], 32 * (o // 2 + 1))
                        dve.tensor_tensor(obuf[:, o % 2, 0:512], bank[7][:, :],
                                          zmem[:, o % 2, :, :].rearrange("p h n -> p (h n)"), ALU.mult).then_inc(s_o, 1)
                    elif u[3] == 1:
                        dve.wait_ge(s_pv, a + 1)
                        dve.wait_ge(s_exp, a + 1)
                        dve.tensor_copy(obuf[:, o % 2, 0:AW], bank[7][:, :]).then_inc(s_o, 1)
                elif s[0] == "merge":
                    b = s[1]
                    sl = b % 2
                    top, tot = mo[:, sl, :, AW:AW + HEADS], mo[:, sl, :, AW + HEADS:]
                    if b == 0:
                        merge_free(dve)
                    dve.wait_ge(s_mgl[sl], 64 * (b // 2 + 1))
                    d = mw[:, 0:24].rearrange("p (g h) -> p g h", g=NG)
                    e = mw[:, 32:56].rearrange("p (g h) -> p g h", g=NG)
                    le = mw[:, 64:88].rearrange("p (g h) -> p g h", g=NG)
                    mm, r = mw[:, 96:104], mw[:, 104:112]
                    link(dve.tensor_tensor(mm, top[:, 0, :], top[:, 1, :], ALU.max))
                    link(dve.tensor_tensor(mm, mm, top[:, 2, :], ALU.max))
                    dve.tensor_tensor(d, top, mm.unsqueeze(1).broadcast_to([P, NG, HEADS]), ALU.subtract).then_inc(s_mgm, 1)
                    dve.wait_ge(s_mgx, b + 1)
                    link(dve.tensor_tensor(le, tot, e, ALU.mult))
                    link(dve.tensor_tensor(r, le[:, 0, :], le[:, 1, :], ALU.add))
                    link(dve.tensor_tensor(r, r, le[:, 2, :], ALU.add))
                    link(dve.reciprocal(r, r))
                    link(dve.tensor_tensor(le, e, r.unsqueeze(1).broadcast_to([P, NG, HEADS]), ALU.mult))
                    if b >= 2:
                        dve.wait_ge(s_mgt, b - 1)
                    acc = macc[:, sl, :].rearrange("p (h d) -> p h d", h=HEADS)
                    tmp = mtmp[:, :].rearrange("p (h d) -> p h d", h=HEADS)
                    for g in range(NG):
                        o = mo[:, sl, g, 0:AW].rearrange("p (h d) -> p h d", h=HEADS)
                        w = le[:, g, :].unsqueeze(2).broadcast_to([P, HEADS, HD])
                        if g == 0:
                            link(dve.tensor_tensor(acc, o, w, ALU.mult))
                        else:
                            link(dve.tensor_tensor(tmp, o, w, ALU.mult))
                            link(dve.tensor_tensor(acc, acc, tmp, ALU.add))
                    dve.tensor_tensor(macc[:, sl, :], macc[:, sl, :], mz[:, sl, :], ALU.mult).then_inc(s_mgd, 1)
                elif s[0] == "sprep":
                    g = s[1]
                    if g == 0:
                        dve.wait_ge(s_mgt, NB)
                        for i in range(2):
                            dve.wait_ge(s_mgs[i], 16 * 4)
                        dve.wait_ge(s_mgd, NB)
                        link(dve.memset(qbd[:, :, :, :, :], 0.0))
                    dve.wait_ge(s_sqt, g + 1)
                    q = bank[5][:, 0:128].rearrange("p (i n) -> p i n", i=4)
                    dve.tensor_copy(qbd[0:64, g, :, :, 0], q[0:64])
                    dve.tensor_copy(qbd[64:128, g, :, :, 1], q[64:128])
                    dve.tensor_copy(kTs[:, g, :, :], bank[5][:, 128:256].rearrange("p (i n) -> p i n", i=4)).then_inc(s_sqc, 1)
                elif s[0] == "skey" and s[1] < len(sets) and s[1] % 2 == 1:
                    n = s[1]
                    dve.wait_ge(s_skt, n + 1)
                    if n >= 2:
                        dve.wait_ge(s_sks, n - 1)
                    dve.tensor_copy(kset[:, 1, :, :], bank[6][:, :].rearrange("p (i n) -> p i n", i=4)).then_inc(s_skD, 1)
                elif s == ("ssoft", "att"):
                    a, b_ = CONST_AT["old"]
                    n0 = CONST_AT["new"][0]
                    for half in range(2):
                        row = srow[:, half, :, :]
                        dve.wait_ge(s_sb1, half + 1)
                        old = bank[5][:, 0:384].rearrange("p (g n) -> p g n", g=NG)
                        new = bank[6][:, 0:96].rearrange("p (g n) -> p g n", g=NG)
                        m0 = con[:, n0 + 64 * half:n0 + 64 * half + NS]
                        m1 = con[:, n0 + 64 * half + NS:n0 + 64 * half + 2 * NS]
                        dve.tensor_tensor(row[:, 0, 0:P], old[:, 0, :], con[:, a:b_], ALU.add)
                        dve.tensor_copy(row[:, 1:3, 0:P], old[:, 1:3, :])
                        dve.tensor_tensor(row[:, 0, P:], new[:, 0, :], m0, ALU.add)
                        link(dve.tensor_tensor(row[:, 1:3, P:], new[:, 1:3, :], m1.unsqueeze(1).broadcast_to([P, 2, NS]), ALU.add))
                        flat = row.rearrange("p g n -> p (g n)")
                        link(dve.tensor_reduce(sstat[:, half:half + 1], flat, AX, ALU.max))
                        dve.tensor_scalar(sstat[:, 2 + half:3 + half], sstat[:, half:half + 1], -(HD ** -0.5), None, ALU.mult).then_inc(s_sm, 1)
                        dve.wait_ge(s_sx, half + 1)
                        link(dve.reciprocal(sstat[:, 6 + half:7 + half], sstat[:, 4 + half:5 + half]))
                        dve.tensor_scalar(flat, flat, sstat[:, 6 + half:7 + half], None, ALU.mult).then_inc(s_sn, 1)
                        dve.wait_ge(s_sb2, half + 1)
                        dve.tensor_copy(pTn[:, :, half, :], bank[6][0:NS, 0:384].rearrange("p (g n) -> p g n", g=NG)).then_inc(s_sc6, 1)
                elif s == ("ssoft", "mem"):
                    dve.wait_ge(s_sb1, 3)
                    link(dve.tensor_copy(mrow, bank[5][:, 0:256]))
                    link(dve.tensor_reduce(sstat[:, 8:9], mrow, AX, ALU.max))
                    dve.tensor_scalar(sstat[:, 9:10], sstat[:, 8:9], -(MD ** -0.5), None, ALU.mult).then_inc(s_sm, 1)
                    dve.wait_ge(s_sx, 3)
                    link(dve.reciprocal(sstat[:, 11:12], sstat[:, 10:11]))
                    dve.tensor_scalar(mrow, mrow, sstat[:, 11:12], None, ALU.mult).then_inc(s_sn, 1)
                    dve.wait_ge(s_sb2, 3)
                    dve.tensor_copy(mP, bank[6][:, 0:256]).then_inc(s_sc6, 1)
                elif s[0] == "sout":
                    zT = soft[:, 1, 0, 0:P].rearrange("p (i n) -> p i n", i=4)
                    dve.wait_ge(s_szt, 1)
                    link(dve.tensor_copy(zT, bank[5][:, 0:P].rearrange("p (i n) -> p i n", i=4)))
                    dve.wait_ge(s_sv, len(sets))
                    dve.wait_ge(s_spz, 16 * 9)
                    wait_part1_stores(dve)
                    o = bank[3][:, 0:256].rearrange("p (b i t e) -> p i b t e", b=BS, i=4, t=TS)
                    for e in range(2):
                        r = slice(64 * e, 64 * e + 64)
                        for i in range(4):
                            dve.tensor_tensor(ysam[r, 0, i, :].rearrange("p (b t) -> p b t", b=BS), o[r, i, :, :, e],
                                              zT[r, i, :].rearrange("p (b t) -> p b t", b=BS), ALU.mult)
                    dve.tensor_tensor(ysam[:, 1, :, :], bank[4][:, 0:P].rearrange("p (h n) -> p h n", h=MH), mzs, ALU.mult).then_inc(s_so, 1)
                elif s[0] == "ssd_setup":
                    late_free(dve)
                    dve.wait_ge(s_s0a, 1)
                    dve.wait_ge(s_dte, 1)
                    bc = lambda i: hrow[:, i, :].unsqueeze(1).broadcast_to([P, 9, SH])
                    v3 = lambda i: sc[:, i, :].rearrange("p (c h) -> p c h", h=SH)
                    link(dve.tensor_tensor(v3(8), dtv[:, :].rearrange("p (c h) -> p c h", h=SH), bc(0), ALU.add))
                    link(dve.tensor_scalar(sc[:, 7, :], sc[:, 8, :], -1.0, None, ALU.mult))
                    dve.tensor_tensor(sc[:, 7, :], sc[:, 7, :], sc[:, 8, :], ALU.max).then_inc(s_s0, 1)
                    dve.wait_ge(s_s0a, 2)
                    dve.tensor_scalar(sc[:, 7, :], sc[:, 9, :], 1.0, None, ALU.add).then_inc(s_s0, 1)
                    dve.wait_ge(s_s0, 2)
                    link(dve.tensor_scalar(sc[:, 5, :], sc[:, 7, :], -1.0, None, ALU.add))
                    link(dve.tensor_tensor(sc[:, 5, :], sc[:, 9, :], sc[:, 5, :], ALU.subtract))
                    link(dve.reciprocal(sc[:, 6, :], sc[:, 7, :]))
                    link(dve.tensor_tensor(sc[:, 5, :], sc[:, 5, :], sc[:, 6, :], ALU.mult))
                    dve.wait_ge(s_s0a, 3)
                    link(dve.tensor_tensor(sc[:, 5, :], sc[:, 5, :], sc[:, 4, :], ALU.add))
                    link(dve.scalar_tensor_tensor(sc[:, 0, :], sc[:, 8, :], 0.0, sc[:, 5, :], ALU.max, ALU.add))
                    link(dve.tensor_tensor(v3(1), v3(0), bc(1), ALU.mult))
                    link(dve.tensor_scalar(sc[:, 1, :], sc[:, 1, :], -1.0, None, ALU.mult))
                    link(dve.tensor_copy(yo[0:NS, :].rearrange("p (h d) -> p h d", h=SH),
                                         sc[0:NS, 1, P:].unsqueeze(2).broadcast_to([NS, SH, SP])))
                    dve.memset(state[:, :], 0.0).then_inc(s_s0, 1)
                    dve.wait_ge(s_s0p, 1)
                    dve.tensor_copy(sc[:, 2, 0:P], bank[6][:, 0:P])
                    dve.tensor_copy(sc[0:NS, 2, P:], bank[6][0:NS, P:144])
                    dve.tensor_copy(sc[:, 5, 0:P], bank[6][:, 256:384])
                    dve.tensor_copy(sc[0:NS, 5, P:], bank[6][0:NS, 384:400])
                    link(dve.tensor_copy(cdraw, bank[7][:, 0:64]))
                    dve.tensor_tensor(sc[:, 4, 0:P], sc[:, 5, 0:P], sc[:, 2, 0:P], ALU.subtract)
                    dve.tensor_tensor(sc[0:NS, 4, P:], sc[0:NS, 5, P:], sc[0:NS, 2, P:], ALU.subtract).then_inc(s_s0, 1)
                    dve.wait_ge(s_s0a, 4)
                    dve.tensor_tensor(sc[:, 6, 0:P], sc[:, 0, 0:P], sc[:, 4, 0:P], ALU.mult)
                    link(dve.tensor_tensor(sc[0:NS, 6, P:], sc[0:NS, 0, P:], sc[0:NS, 4, P:], ALU.mult))
                elif s[0] == "ya":
                    k = s[1]
                    dve.wait_ge(s_yah, k + 1)
                    dve.tensor_tensor(yAl[:, k, :], ya_slot(k), yAh[:, k, :].bitcast(F32), ALU.subtract).then_inc(s_yal, 1)
                elif s[0] == "yb":
                    k = s[1]
                    dve.wait_ge(s_yah, KT8 + k + 1)
                    dve.tensor_tensor(yBl[:, k, :], yb_slot(k), yBh[:, k, :].bitcast(F32), ALU.subtract).then_inc(s_yal, 1)
                elif s[0] == "p1":
                    _, n, f, br, j = s
                    ft = chunks[n][1] + f
                    u = proj[s]
                    cols = slice(THIRD * j, THIRD * j + THIRD)
                    dve.wait_ge(s_pj, u + 1)
                    dve.wait_ge(s_g1, 32 * (ft + 1))
                    psum = bank[u % 3][:, 0:THIRD]
                    if br == 0:
                        if ft and j == 0:
                            dve.wait_ge(s_p1st, 16 * ft)
                        elif j == 0:
                            dve.wait_ge(s_yal, KT8)
                        dve.tensor_tensor(acc1[:, cols], psum, gate1[:, 0, cols], ALU.mult).then_inc(s_pjv, 1)
                    else:
                        dve.tensor_tensor(gate1[:, 1, cols], psum, gate1[:, 1, cols], ALU.mult).then_inc(s_pjv, 1)
                        dve.wait_ge(s_pjv, u - n_act_proj + 1)
                        ins = dve.tensor_tensor(acc1[:, cols], acc1[:, cols], gate1[:, 1, cols], ALU.add)
                        if j == 2:
                            ins.then_inc(s_p1, 1)
                            dve.wait_ge(s_p1, ft + 1)
                elif s[0] == "p2":
                    _, n, f, j = s
                    ft = chunks[n][1] + f
                    u = proj[s]
                    x = 3 * ft + j
                    cols = slice(THIRD * j, THIRD * j + THIRD)
                    dve.wait_ge(s_pj, u + 1)
                    dve.wait_ge(s_g1, 32 * KT8 + 32 * (ft + 1))
                    if x >= 3:
                        dve.wait_ge(s_ml, x - 2)
                    dve.tensor_tensor(yraw2[:, cols], bank[u % 3][:, 0:THIRD], gate2[:, cols], ALU.mult).then_inc(s_pjv, 1)
                    dve.wait_ge(s_pjv, u - n_act_proj + 1)
                    dve.tensor_tensor(yraw2[:, cols], yraw2[:, cols], acc2[:, cols], ALU.add).then_inc(s_m, 1)
                    dve.wait_ge(s_mh, x + 1)
                    ins = dve.tensor_tensor(mTl[:, ft, cols], yraw2[:, cols], mTh[:, ft, cols].bitcast(F32), ALU.subtract).then_inc(s_ml, 1)
                elif s[0] == "ssd":
                    _, c, q = s
                    m = P if c < NB else NS
                    h0 = SH * c
                    per_head = lambda k: sc[0:m, k, h0:h0 + SH].unsqueeze(2).broadcast_to([m, SH, SP])
                    heads = lambda t: t[0:m, :].rearrange("p (h d) -> p h d", h=SH)
                    if q == 0:
                        dve.wait_ge(s_db, c + 1)
                        if c >= 1:
                            dve.wait_ge(s_dM, 4 * c)
                        up = (table("upper") if c < NB else table("upper_s"))[0:m, 0:m]
                        dve.tensor_tensor(CBm[0:m, :, 0:m], bank[6][0:m, 0:4 * m].rearrange("p (g n) -> p g n", g=SG),
                                          up.unsqueeze(1).broadcast_to([m, SG, m]), ALU.mult).then_inc(s_dcb, 1)
                        dve.wait_ge(s_dxt, c + 1)
                        if c >= 1:
                            dve.wait_ge(s_dy, c)
                            if c < NB:
                                dve.wait_ge(s_ds, 2 * c)
                        dve.tensor_tensor(heads(xdt), heads(xtok), per_head(0), ALU.mult)
                        if c == NB:
                            dve.wait_ge(s_ds, 2 * NB)
                        dve.tensor_tensor(heads(xdec), heads(xtok), per_head(6), ALU.mult).then_inc(s_dxd, 1)
                    elif q in (1, 2):
                        for qq in (2 * q - 2, 2 * q - 1):
                            dve.wait_ge(s_dD, 4 * c + qq + 1)
                            if qq == 0 and c == NB:
                                dve.wait_ge(s_fst8, 16)
                            for h in range(4):
                                ins = dve.tensor_scalar(Lm_of(c, qq)[:, h, :], D_of(c, qq)[:, h, :],
                                                        sc[0:m, 2, h0 + 4 * qq + h:h0 + 4 * qq + h + 1], 0.0,
                                                        ALU.subtract, ALU.min)
                            ins.then_inc(s_ddf, 1)
                            dve.wait_ge(s_dL, 4 * c + qq + 1)
                            if qq == 0:
                                dve.wait_ge(s_dcb, c + 1)
                            l = Lm_of(c, qq)
                            dve.tensor_tensor(l, l, CBm[0:m, qq, 0:m].unsqueeze(1).broadcast_to([m, 4, m]), ALU.mult).then_inc(s_dM, 1)
                    elif q == 4:
                        oa, ob = (3, 4) if c < NB else (0, 1)
                        if c < NB:
                            dve.wait_ge(s_do, c + 1)
                        else:
                            dve.wait_ge(s_eo, BS)
                        if c:
                            dve.wait_ge(s_xt, n_norm + c)
                            dve.wait_ge(s_sq, n_norm + c)
                        for i, o in enumerate((oa, ob)):
                            ins = dve.tensor_tensor(yo[0:m, 512 * i:512 * i + 512].rearrange("p (h d) -> p h d", h=8),
                                                    bank[o][0:m, :].rearrange("p (h d) -> p h d", h=8),
                                                    sc[0:m, 3, h0 + 8 * i:h0 + 8 * i + 8].unsqueeze(2).broadcast_to([m, 8, SP]), ALU.mult)
                        link(ins)
                        for i, o in enumerate((5, 7)):
                            ins = dve.tensor_tensor(yy[0:m, 512 * i:512 * i + 512], bank[o][0:m, :], yo[0:m, 512 * i:512 * i + 512], ALU.add)
                        ins.then_inc(s_dyp, 1)
                        dve.wait_ge(s_dyp, c + 1)
                        link(dve.tensor_tensor(heads(yo), heads(xtok), hrow[0:m, 2, :].unsqueeze(2).broadcast_to([m, SH, SP]), ALU.mult))
                        link(dve.tensor_tensor(yy[0:m, :], yy[0:m, :], yo[0:m, :], ALU.add))
                        dve.tensor_tensor(yy[0:m, :], yy[0:m, :], zt[0:m, :], ALU.mult).then_inc(s_dyd, 1)
                        dve.wait_ge(s_dyd, c + 1)
                        if c < NB:
                            link(dve.tensor_tensor(heads(state), heads(state), per_head(5), ALU.mult))
                            for i in range(2):
                                dve.wait_ge(s_ds, 2 * c + i + 1)
                                dve.tensor_tensor(state[:, 512 * i:512 * i + 512], state[:, 512 * i:512 * i + 512],
                                                  bank[6][:, :], ALU.add).then_inc(s_dsn, 1)
                    elif q == 5:
                        r = small[0:m, 32 + c:33 + c]
                        dve.wait_ge(s_sq, n_norm + c + 1)
                        link(dve.tensor_scalar(r, r, 1.0 / D, EPS, ALU.mult, ALU.add))
                        dve.reciprocal(r, r).then_inc(s_var, 1)
                        dve.wait_ge(s_rstd, n_norm + c + 1)
                        if c == 0:
                            dve.wait_ge(s_sw, 16)
                        dve.scalar_tensor_tensor(yy[0:m, :], yy[0:m, :], r, ssdw[0:m, :], ALU.mult, ALU.mult).then_inc(s_xn, 1)
                elif s[0] == "ssd_s":
                    dve.wait_ge(s_p1st, 16 * KT8)
                    link(dve.memset(gate1[:, 0, 0:D], 0.0))
                    dve.wait_ge(s_xc, 32 * (NB + 1))
                    for b in range(BS):
                        ins = dve.tensor_copy(cmask[:, :, b, TS * b:TS * b + TS], xcs[:, 12:16, TS * b:TS * b + TS])
                    ins.then_inc(s_ecm, 1)
                elif s[0] == "ssd_sb":
                    b = s[1]
                    if b == 0:
                        dve.wait_ge(s_dbt, NB + 1)
                    if b >= 2:
                        dve.wait_ge(s_es, b - 1)
                    dve.tensor_scalar(btb(b), btok[0:NS, :], table("same_b")[0:NS, b:b + 1], None, ALU.mult).then_inc(s_eb, 1)
                    dve.wait_ge(s_es, b + 1)
                    if b >= 1:
                        dve.wait_ge(s_est, 16 * b)
                    new = Lflat[:, D:2 * D].rearrange("p (i n) -> p i n", i=8)
                    for i in range(8):
                        ins = dve.scalar_tensor_tensor(new[:, i, :], prev_slot(b)[:, i, :], cdcol[:, 8 * i + b:8 * i + b + 1],
                                                       bank[6 if i < 4 else 2][:, P * (i % 4):P * (i % 4) + P], ALU.mult, ALU.add)
                    ins.then_inc(s_en, 1)
                elif s[0] == "out":
                    _, n, t = s
                    x, u = out_no[s], proj[s]
                    m = P if t < NB else NS
                    dve.wait_ge(s_pj, u + 1)
                    dve.wait_ge(s_xr[x % 4], 16 * (x // 4 + 1))
                    c0 = CW * chunks[n][1]
                    dve.tensor_tensor(orows[0:m, t, c0:c0 + CW], bank[u % 3][0:m, 0:CW], xres[0:m, x % 4, :], ALU.add).then_inc(s_pjv, 1)
                    if chunks[n][1] == 3:
                        r = small[0:m, 44 + t:45 + t]
                        dve.wait_ge(s_sq, n_norm + NB + 1 + t + 1)
                        link(dve.tensor_scalar(r, r, 1.0 / D, EPS, ALU.mult, ALU.add))
                        dve.reciprocal(r, r).then_inc(s_var, 1)
                        dve.wait_ge(s_rstd, n_norm + NB + 1 + t + 1)
                        dve.wait_ge(s_nf, 16)
                        dve.scalar_tensor_tensor(orows[0:m, t, :], orows[0:m, t, :], r, normf[0:m, :], ALU.mult, ALU.mult).then_inc(s_xn, 1)

        @block.tensor
        def _(pe):
            ident = table("ident")
            pe.wait_ge(s_const, 48)

            def bank_free(u):
                if u >= 3:
                    pe.wait_ge(s_pjev, u - 2)

            def three(out, xh, xl, wh, wl, nk, signal=None):
                for k in range(nk):
                    pe.matmul(out, xh(k), wh(k), start=(k == 0), stop=False)
                    pe.matmul(out, xh(k), wl(k), start=False, stop=False)
                    ins = pe.matmul(out, xl(k), wh(k), start=False, stop=(k == nk - 1))
                return ins

            started = set()
            for s in sched:
                if s[0] == "norm_b":
                    i = s[1]
                    m = P if i < 10 else NS
                    pe.wait_ge(s_xn, i + 1)
                    if i >= 2:
                        pe.wait_ge(s_hlo, 2 * i - 2)
                    if turns_before[s]:
                        pe.wait_ge(s_turned, turns_before[s])
                    for k in range(KT8):
                        ins = pe.transpose(bank[3 + 2 * (i % 2) + k // 4][:, P * (k % 4):P * (k % 4) + m],
                                           xin[0:m, i % 2, P * k:P * k + P], ident[0:m, 0:m])
                    ins.then_inc(s_xt, 1)
                elif s[0] == "dt":
                    pe.wait_ge(s_wdtl, 1)
                    pe.wait_ge(s_hlo, 2 * n_norm)
                    pe.wait_ge(s_cv, 16 * 9)
                    pe.transpose(bank[7][:, 0:80], obuf[0:80, 0, 0:P], ident[0:80, 0:80]).then_inc(s_cvt, 1)
                    for f in range(16):
                        src = softT[0:24, f // 8, 2 * (f // 4 % 2):2 * (f // 4 % 2) + 2, :, :].rearrange("p a b n -> p (a b) n")[:, f % 4, :]
                        ins = pe.transpose(bank[4][:, 24 * f:24 * f + 24], src, ident[0:24, 0:24])
                    ins.then_inc(s_cvt, 1)
                    for t in range(NB + 1):
                        m = P if t < NB else NS
                        c0 = P * t
                        ins = three(bank[3][0:m, SH * t:SH * t + SH],
                                    lambda k: hTh[:, k, c0:c0 + m], lambda k: hTl[:, k, c0:c0 + m],
                                    lambda k: wdt_hi[:, k, :], lambda k: wdt_lo[:, k, :], KT8)
                    ins.then_inc(s_dtp, 1)
                elif s[0] in ("tok", "feat"):
                    n = s[1]
                    slot = n % 2
                    u = proj[s]
                    if n not in started:
                        started.add(n)
                        pe.wait_ge(s_wlo, n + 1)
                    bank_free(u)
                    if s[0] == "tok":
                        t = s[2]
                        kind, detail = chunks[n][0], chunks[n][1]
                        m = P if t < NB else NS
                        if kind in ("mk", "mv"):
                            pe.wait_ge(s_hlo, 4)
                            xh = lambda k: memTh[:, k, P * t:P * t + P]
                            xl = lambda k: memTl[:, k, P * t:P * t + P]
                        elif t == NB:
                            xh = lambda k: hTh[:, k, SEQ:TOK]
                            xl = lambda k: hTl[:, k, SEQ:TOK]
                        else:
                            g = detail[0] if kind in "qkv" else 0
                            xh = lambda k: token_cols(hTh, k, g, t)
                            xl = lambda k: token_cols(hTl, k, g, t)
                        ins = three(bank[u % 3][0:m, 0:CW], xh, xl,
                                    lambda k: w_hi[:, slot, k, :], lambda k: w_lo[:, slot, k, :], KT8)
                    else:
                        f, j = s[2], s[3]
                        ins = three(bank[u % 3][:, 0:THIRD],
                                    lambda k: w_hi[:, slot, k, P * f:P * f + P], lambda k: w_lo[:, slot, k, P * f:P * f + P],
                                    lambda k: hTh[:, k, THIRD * j:THIRD * j + THIRD], lambda k: hTl[:, k, THIRD * j:THIRD * j + THIRD], KT8)
                    ins.then_inc(s_pj, 1)
                elif s[0] == "turn":
                    _, n, t = s
                    v = turned[s]
                    c = slot_of[("tok", n, t)]
                    kind = chunks[n][0]
                    if kind == "mk":
                        pe.wait_ge(s_pjev, proj[("tok", n, t)] + 1)
                    else:
                        pe.wait_ge(s_rope, roped[("tok", n, t)] + 1)
                        g = chunks[n][1][0]
                        if t == 0:
                            pe.wait_ge(s_ptD, first_att[g])
                            pe.wait_ge(s_ptA, first_att[g])
                    if v >= 2:
                        pe.wait_ge(s_turned, v - 1)
                    if kind == "mk":
                        pe.wait_ge(s_hlo, 2 * norms_before[s])
                    for i in range(2):
                        ins = pe.transpose(bank[5 + v % 2][:, P * i:P * i + P], rows[:, c % 4, P * i:P * i + P], ident)
                    ins.then_inc(s_turn, 1)
                elif s[0] == "scores":
                    a = s[1]
                    u = units[a]
                    kb, _, b0 = keys(a)
                    if a >= 1:
                        pe.wait_ge(s_msk, a)
                    if u[0] == "mem":
                        t = u[1]
                        pe.wait_ge(s_qm[t % 2], 32 * (t // 2 + 1))
                        if a == 0:
                            pe.wait_ge(s_turned, 4)
                            pe.wait_ge(s_dte, 1)
                        for h in range(4):
                            ins = pe.matmul(bank[3 + h % 2][:, CW * (h // 2):CW * (h // 2) + CW],
                                            qmem[:, t % 2, h, :], KmT[:, h, :], start=True, stop=True)
                    else:
                        _, g, b, half = u
                        if a == first_att[g]:
                            pe.wait_ge(s_turned, 4 + (g + 1) * 4 * NB)
                        for h in range(4):
                            i, r = 2 * half + h // 2, 64 * (h % 2)
                            ins = pe.matmul(bank[3 + h % 2][:, CW * (h // 2):CW * (h // 2) + kb * P],
                                            QT[r:r + 64, i, P * b:P * b + P], KTt[r:r + 64, i, P * b0:P * (b0 + kb)],
                                            start=True, stop=True)
                    ins.then_inc(s_sc, 1)
                elif s[0] == "ptrans":
                    a = s[1]
                    kb = keys(a)[0]
                    if units[a][0] == "mem":
                        pe.wait_ge(s_pn, a + 1)
                    else:
                        pe.wait_ge(s_exp, a + 1)
                    if a >= 1:
                        pe.wait_ge(s_ptA, a)
                        pe.wait_ge(s_ptD, a)
                    if units[a][0] == "mem" or a == first_att[units[a][1]]:
                        pe.wait_ge(s_turned, 4 if units[a][0] == "mem" else 4 + (units[a][1] + 1) * 4 * NB)
                    for h in range(4):
                        for k in range(kb):
                            c0 = ((h % 2) * kb + k) * P
                            ins = pe.transpose(bank[5 + h // 2][:, c0:c0 + P], soft[:, a % 2, h, P * k:P * k + P], ident)
                    ins.then_inc(s_pt, 1)
                elif s[0] == "pv":
                    a = s[1]
                    u = units[a]
                    kb, _, b0 = keys(a)
                    o = o_use[a]
                    pe.wait_ge(s_ptA, a + 1)
                    pe.wait_ge(s_ptD, a + 1)
                    if (u[0] == "mem" or u[3] == 0) and o >= 1:
                        pe.wait_ge(s_o, o)
                    if u[0] == "mem":
                        if a == 0:
                            pe.wait_ge(s_cvc, 2)
                        for h in range(4):
                            for k in range(2):
                                ins = pe.matmul(bank[7][:, P * h:P * h + P], Vm[:, k, MD * h:MD * h + MD],
                                                softT[:, a % 2, h, k, :], start=(k == 0), stop=(k == 1))
                    else:
                        _, g, b, half = u
                        if a == first_att[g]:
                            pe.wait_ge(s_pjev, max(v for s_, v in proj.items() if chunks[s_[1]][0] == "v" and chunks[s_[1]][1][0] == g) + 1)
                        for h in range(4):
                            c0 = (4 * half + h) * HD
                            for k in range(kb):
                                ins = pe.matmul(bank[7][:, c0:c0 + HD], softT[:, a % 2, h, k, :],
                                                V[:, b0 + k, c0:c0 + HD], start=(k == 0), stop=(k == kb - 1))
                    ins.then_inc(s_pv, 1)
                elif s[0] == "merge":
                    b = s[1]
                    if b == 0:
                        pe.wait_ge(s_msk, len(units))
                    if b >= 2:
                        pe.wait_ge(s_mge, b - 1)
                    pe.wait_ge(s_mgd, b + 1)
                    for i in range(4):
                        ins = pe.transpose(bank[3 + b % 2][:, P * i:P * i + P], macc[:, b % 2, P * i:P * i + P], ident)
                    ins.then_inc(s_mgt, 1)
                elif s[0] == "sprep":
                    g = s[1]
                    pe.wait_ge(s_sp, 32 * (g + 1))
                    if g == 0:
                        pe.wait_ge(s_ptA, len(units))
                        pe.wait_ge(s_ptD, len(units))
                        pe.wait_ge(s_o, o_count)
                        pe.wait_ge(s_mge, NB)
                    else:
                        pe.wait_ge(s_sqc, g)
                    for j in range(2):
                        for i in range(4):
                            c0 = P * j + NS * i
                            ins = pe.transpose(bank[5][:, c0:c0 + NS], qkS[:, j, P * i:P * i + P], ident[0:NS, 0:NS])
                    ins.then_inc(s_sqt, 1)
                    pe.wait_ge(s_sqc, g + 1)
                    if g:
                        pe.wait_ge(s_snc, g)
                    for i in range(4):
                        ins = pe.matmul(bank[7][0:NS, 0:256].rearrange("p (n h) -> p n h", h=8)[:, :, 2 * i:2 * i + 2],
                                        kTs[:, g, i, :], qbd[:, g, i, :, :], start=True, stop=True)
                    ins.then_inc(s_snp, 1)
                elif s[0] == "skey":
                    n = s[1]
                    if n < len(sets):
                        pe.wait_ge(s_kv[n % NRING], 16 * (n // NRING + 1))
                        if n == 0:
                            pe.wait_ge(s_snc, NG)
                            pe.wait_ge(s_spz, 16 * 9)
                        if n >= 2:
                            pe.wait_ge(s_skA if n % 2 == 0 else s_skD, n // 2)
                        for i in range(4):
                            ins = pe.transpose(bank[5 + n % 2][:, P * i:P * i + P], kvring[:, n % NRING, P * i:P * i + P], ident)
                        ins.then_inc(s_skt, 1)
                    if n >= 1:
                        m = n - 1
                        kind, b, g, t = sets[m]
                        pe.wait_ge(s_skA if m % 2 == 0 else s_skD, m // 2 + 1)
                        for i in range(4):
                            if kind == "mem":
                                out = bank[7][:, P * g:P * g + P].rearrange("p (b t h) -> p b t h", t=TS, h=MH)[:, b, :, i]
                                rhs = mq[:, i, TS * b:TS * b + TS]
                            else:
                                dst = bank[4 if g == 2 else 3][:, 256 * (g % 2):256 * (g % 2) + 256].rearrange("p (n h) -> p n h", h=8)
                                ns = slice(TS * b, TS * b + TS) if t is None else slice(TS * b + t, TS * b + t + 1)
                                out = dst[:, ns, 2 * i:2 * i + 2]
                                rhs = qbd[:, g, i, ns, :]
                            ins = pe.matmul(out, kset[:, m % 2, i, :], rhs, start=True, stop=True)
                        ins.then_inc(s_sks, 1)
                elif s == ("ssoft", "att"):
                    pe.wait_ge(s_sa, 1)
                    pe.wait_ge(s_skA, (len(sets) + 1) // 2)
                    pe.wait_ge(s_skD, len(sets) // 2)
                    for half in range(2):
                        for g in range(NG):
                            pe.transpose(bank[5][:, P * g:P * g + P], sT[:, g, P * half:P * half + P], ident)
                            ins = pe.transpose(bank[6][:, NS * g:NS * g + NS], sTn[:, g, P * half:P * half + P], ident[0:NS, 0:NS])
                        ins.then_inc(s_sb1, 1)
                        pe.wait_ge(s_sn, half + 1)
                        for g in range(NG):
                            pe.transpose(bank[5][:, P * g:P * g + P], srow[:, half, g, 0:P], ident)
                            ins = pe.transpose(bank[6][0:NS, P * g:P * g + P], srow[:, half, g, P:], ident)
                        ins.then_inc(s_sb2, 1)
                        pe.wait_ge(s_sc5, half + 1)
                        pe.wait_ge(s_sc6, half + 1)
                elif s == ("ssoft", "mem"):
                    for k in range(2):
                        ins = pe.transpose(bank[5][:, P * k:P * k + P], mS[:, P * k:P * k + P], ident)
                    ins.then_inc(s_sb1, 1)
                    pe.wait_ge(s_sn, 3)
                    for k in range(2):
                        ins = pe.transpose(bank[6][:, P * k:P * k + P], mrow[:, P * k:P * k + P], ident)
                    ins.then_inc(s_sb2, 1)
                elif s[0] == "sval":
                    n = s[1]
                    q = len(sets) + n
                    kind, b, g, t = sets[n]
                    if n == 0:
                        pe.wait_ge(s_sc6, 3)
                    pe.wait_ge(s_kv[q % NRING], 16 * (q // NRING + 1))
                    half, r0 = b // 4, 32 * (b % 4)
                    if kind == "att":
                        dst = bank[3][:, 0:256].rearrange("p (b i t e) -> p b i t e", b=BS, i=4, t=TS)[:, b]
                        if g == 0:
                            for g2 in range(NG):
                                p = pTn[:, g2, half, r0:r0 + 32].rearrange("p (t h) -> p t h", h=8)
                                for i in range(4):
                                    pe.matmul(dst[:, i], vS[:, g2, P * i:P * i + P], p[:, :, 2 * i:2 * i + 2],
                                              start=(g2 == 0 and i == 0), stop=False, skip_group_check=True)
                        p = pT[:, g, half, r0:r0 + 32].rearrange("p (t h) -> p t h", h=8)
                        ts = slice(0, TS) if t is None else slice(t, t + 1)
                        for i in range(4):
                            ins = pe.matmul(dst[:, i, ts, :], kvring[:, q % NRING, P * i:P * i + P], p[:, ts, 2 * i:2 * i + 2],
                                            start=False, stop=(g == 2 and t == TS - 1 and i == 3), skip_group_check=True)
                    else:
                        for i in range(4):
                            ins = pe.matmul(bank[4][:, NS * i + TS * b:NS * i + TS * b + TS], kvring[:, q % NRING, P * i:P * i + P],
                                            mP[:, P * g:P * g + P].rearrange("p (b t h) -> p b t h", t=TS, h=MH)[:, b, :, i],
                                            start=(g == 0 and i == 0), stop=(g == 1 and i == 3), skip_group_check=True)
                    ins.then_inc(s_sv, 1)
                elif s[0] == "sout":
                    for i in range(4):
                        ins = pe.transpose(bank[5][:, NS * i:NS * i + NS], zas[0:NS, P * i:P * i + P], ident[0:NS, 0:NS])
                    ins.then_inc(s_szt, 1)
                elif s[0] == "ssd_setup":
                    pe.wait_ge(s_s0, 3)
                    dA = sc[:, 1, :]
                    pe.matmul(bank[6][:, 0:P], table("upper"), dA[:, 0:P], start=True, stop=True)
                    pe.matmul(bank[6][0:NS, P:144], table("upper_s")[0:NS, :], dA[0:NS, P:], start=True, stop=True)
                    pe.matmul(bank[6][:, 256:384], table("ones"), dA[:, 0:P], start=True, stop=True)
                    pe.matmul(bank[6][0:NS, 384:400], table("same_s")[0:NS, :], dA[0:NS, P:], start=True, stop=True)
                    for i in range(8):
                        ins = pe.matmul(bank[7][:, 8 * i:8 * i + 8], yo[0:NS, P * i:P * i + P], table("same_b")[0:NS, :], start=True, stop=True)
                    ins.then_inc(s_s0p, 1)
                elif s[0] in ("p1", "p2", "out"):
                    n = s[1]
                    slot = n % 2
                    u = proj[s]
                    if n not in started:
                        started.add(n)
                        pe.wait_ge(s_wlo, n + 1)
                    if s[0] == "p1" and u == n_act_proj:
                        pe.wait_ge(s_yal, KT8)
                    if s[0] == "p2" and s[2:] == (0, 0) and chunks[n][1] == 0:
                        pe.wait_ge(s_yal, KT8 + KT8)
                        pe.wait_ge(s_tle, 4)
                    if s[0] == "out" and out_no[s] == 0:
                        pe.wait_ge(s_ml, 3 * KT8)
                    if u - 3 < n_act_proj:
                        pe.wait_ge(s_pjev, u - 2)
                    else:
                        pe.wait_ge(s_pjv, u - 2 - n_act_proj)
                    if s[0] == "out":
                        t = s[2]
                        m = P if t < NB else NS
                        c0 = P * t
                        ins = three(bank[u % 3][0:m, 0:CW], lambda k: mTh[:, k, c0:c0 + m], lambda k: mTl[:, k, c0:c0 + m],
                                    lambda k: w_hi[:, slot, k, :], lambda k: w_lo[:, slot, k, :], KT8)
                    else:
                        f, j = s[2], s[-1]
                        k0 = 4 * s[3] if s[0] == "p1" else 0
                        yh, yl = (yAh, yAl) if s[0] == "p1" else (yBh, yBl)
                        ins = three(bank[u % 3][:, 0:THIRD],
                                    lambda k: w_hi[:, slot, k0 + k, P * f:P * f + P], lambda k: w_lo[:, slot, k0 + k, P * f:P * f + P],
                                    lambda k: yh[:, k0 + k, THIRD * j:THIRD * j + THIRD], lambda k: yl[:, k0 + k, THIRD * j:THIRD * j + THIRD],
                                    4 if s[0] == "p1" else KT8)
                    ins.then_inc(s_pj, 1)
                elif s[0] == "ssd":
                    _, c, q = s
                    m = P if c < NB else NS
                    h0 = SH * c
                    x = xc if c < NB else xcs
                    if q == 0:
                        pe.wait_ge(s_xc, 32 * (c + 1))
                        if c == 0:
                            pe.wait_ge(s_s0, 4)
                        else:
                            pe.wait_ge(s_dys, c)
                            pe.wait_ge(s_dyp, c)
                            pe.wait_ge(s_dsn, 2 * min(c, NB))
                            if c == NB:
                                pe.wait_ge(s_fs, 2)
                        for f in range(8):
                            ins = pe.transpose(bank[3 + f // 4][0:m, P * (f % 4):P * (f % 4) + P], x[:, f, 0:m], ident)
                        ins.then_inc(s_dt, 1)
                        for f in range(4):
                            pe.transpose(bank[5][0:m, P * f:P * f + P], x[:, 8 + f, 0:m], ident)
                        for g in range(SG):
                            ins = pe.matmul(bank[6][0:m, m * g:m * g + m], x[:, 8 + g, 0:m], x[:, 12 + g, 0:m], start=True, stop=True)
                        ins.then_inc(s_db, 1)
                    elif q in (1, 2):
                        up = (table("upper") if c < NB else table("upper_s"))[0:m, 0:m]
                        for qq in (2 * q - 2, 2 * q - 1):
                            if qq == 0:
                                pe.wait_ge(s_dxt, c + 1)
                            if qq >= 2:
                                pe.wait_ge(s_ddf, 4 * c + qq - 1)
                            for h in range(4):
                                col = h0 + 4 * qq + h
                                ins = pe.matmul(D_of(c, qq)[:, h, :], sc[0:m, 1, col:col + 1].broadcast_to([m, m]), up, start=True, stop=True)
                            ins.then_inc(s_dD, 1)
                    elif q == 3:
                        pe.wait_ge(s_dM, 4 * c + 4)
                        pe.wait_ge(s_dxd, c + 1)
                        pe.wait_ge(s_dbt, c + 1)
                        for h in range(SH):
                            ins = pe.matmul(bank[5 if h < 8 else 7][0:m, SP * (h % 8):SP * (h % 8) + SP],
                                            Lm_of(c, h // 4)[:, h % 4, :], xdt[0:m, SP * h:SP * h + SP], start=True, stop=True)
                        ins.then_inc(s_dy, 1)
                        if c < NB:
                            if c:
                                pe.wait_ge(s_dsn, 2 * c)
                            for g in range(SG):
                                ins = pe.matmul(bank[3 + g // 2][:, 256 * (g % 2):256 * (g % 2) + 256], x[:, 12 + g, :],
                                                state[:, 256 * g:256 * g + 256], start=True, stop=True)
                            ins.then_inc(s_do, 1)
                    elif q == 4 and c < NB:
                        for i in range(2):
                            if i == 0:
                                pe.wait_ge(s_dcb, c + 1)
                            else:
                                pe.wait_ge(s_dsn, 2 * c + 1)
                            for g in (2 * i, 2 * i + 1):
                                ins = pe.matmul(bank[6][:, 256 * (g % 2):256 * (g % 2) + 256], btok[:, P * g:P * g + P],
                                                xdec[:, 256 * g:256 * g + 256], start=True, stop=True)
                            ins.then_inc(s_ds, 1)
                    elif q == 5:
                        pe.wait_ge(s_xn, n_norm + c + 1)
                        if c == NB:
                            pe.wait_ge(s_ec, BS)
                        for k in range(8):
                            ins = pe.transpose(bank[3 + k // 4][:, P * (k % 4):P * (k % 4) + m], yy[0:m, P * k:P * k + P], ident[0:m, 0:m])
                        ins.then_inc(s_xt, 1)
                elif s[0] == "ssd_state":
                    pe.wait_ge(s_dsn, 2 * NB)
                    pe.wait_ge(s_dys, NB)
                    for i in range(8):
                        ins = pe.transpose(bank[3 + i // 4][:, P * (i % 4):P * (i % 4) + P], state[:, P * i:P * i + P], ident)
                    ins.then_inc(s_ft, 1)
                elif s[0] == "ssd_sb":
                    b = s[1]
                    pe.wait_ge(s_eld[b % 2], 16 * (b // 2 + 1))
                    if b:
                        pe.wait_ge(s_ec, b)
                    else:
                        pe.wait_ge(s_ecm, 1)
                        pe.wait_ge(s_ddf, 4 * NB + 4)
                        pe.wait_ge(s_pjv, first_p2)
                    for i in range(8):
                        ins = pe.transpose(bank[3 + i // 4][:, P * (i % 4):P * (i % 4) + P], prev_slot(b)[:, i, :], ident)
                    ins.then_inc(s_et, 1)
                    pe.wait_ge(s_eb, b + 1)
                    if b:
                        pe.wait_ge(s_en, b)
                    else:
                        pe.wait_ge(s_dcb, NB + 1)
                    for i in range(8):
                        ins = pe.matmul(bank[6 if i < 4 else 2][:, P * (i % 4):P * (i % 4) + P], xdec[0:NS, P * i:P * i + P],
                                        btb(b)[:, P * (i // 2):P * (i // 2) + P], start=True, stop=True)
                    ins.then_inc(s_es, 1)
                    pe.wait_ge(s_ec, b + 1)
                    for g in range(SG):
                        ins = pe.matmul(bank[g // 2][0:NS, 256 * (g % 2):256 * (g % 2) + 256], cmask[:, g, b, :],
                                        state[:, 256 * g:256 * g + 256], start=(b == 0 and g % 2 == 0),
                                        stop=(b == BS - 1 and g % 2 == 1), skip_group_check=True)
                    ins.then_inc(s_eo, 1)
                elif s[0] == "tail":
                    pe.wait_ge(s_tl, 16)
                    pe.wait_ge(s_dys, NB + 1)
                    pe.wait_ge(s_dyp, NB + 1)
                    pe.wait_ge(s_en, BS)
                    for f in range(16):
                        ins = pe.transpose(bank[3 + f // 4][0:35, P * (f % 4):P * (f % 4) + P], tails[:, f, :], ident)
                    ins.then_inc(s_tlt, 1)


OUTS = [(1, SEQ, D), (BS, TS, D), (1, 128, 2, HEADS, HD), (1, 512, 2, HEADS, HD), (1, SEQ, 2, HEADS, HD),
        (1, MEM, 2, MH, MD), (1, CONV - 1, CD), (1, SH, SP, SN), (BS, TS, 2, HEADS, HD), (BS, TS, 2, HEADS, HD),
        (BS, TS, 2, HEADS, HD), (BS, CONV - 1, CD), (BS, SH, SP, SN)]


def kernel(**inputs):
    import concourse.bacc as bacc
    from concourse.bass_utils import run_bass_kernel_spmd

    nc = bacc.Bacc("TRN2", target_bir_lowering=False, num_devices=1)
    arrays = {f"in_{name}": np.ascontiguousarray(inputs[name]) for name in NAMES}
    arrays["in_const"] = CONST
    io = {name[3:]: nc.dram_tensor(name, a.shape, mybir.dt.from_np(a.dtype), kind="ExternalInput").ap()
          for name, a in arrays.items()}
    outs = [nc.dram_tensor(f"out_{i}", shape, F32, kind="ExternalOutput").ap() for i, shape in enumerate(OUTS)]
    build_program(nc, io, outs)
    r = run_bass_kernel_spmd(nc, [arrays], core_ids=[0])
    return tuple(r.results[0][f"out_{i}"] for i in range(len(OUTS)))
```
